# Optimizing a Trainium2 kernel written in Bass

```python
import jax, jax.numpy as jnp
from jax import lax
import numpy as np

D_MODEL = 1024
BATCH = 1
SEQ = 1024
DEPTH = 1
DEC_BATCH = 8
DEC_SEQ = 1
PAST_LEN = 2048
PAGE_SIZE = 128

MLA_HEADS = 8
QK_NOPE = 64
QK_ROPE = 32
QK_HEAD = QK_NOPE + QK_ROPE
V_HEAD = 64
Q_LORA = 256
KV_LORA = 256
ROPE_THETA = 10000.0
Q_BLOCK = 128
MLA_SCALE = QK_HEAD ** -0.5
C_CONV = 512
CONV_W = 31
MEM_TOKENS = 256
MEM_HEADS = 4
MEM_HD = 128
MEM_W = MEM_HEADS * MEM_HD
MEM_SCALE = MEM_HD ** -0.5
N_BRANCH = 3
IN_COLS = Q_LORA + KV_LORA + QK_ROPE + 2 * C_CONV + MEM_W + N_BRANCH * D_MODEL
N_EXPERTS = 64
TOP_K = 8
D_EXPERT = 256
D_SHARED = 256
ROUTED_SCALE = 2.5
MOE_BLOCK = 128
EPS = 1e-6

kernel_name = 'mla_conformer_memory_moe_decode_step'

def rms_norm(x, g):
    xf = x.astype(jnp.float32)
    y = xf * lax.rsqrt(jnp.mean(xf * xf, axis=-1, keepdims=True) + EPS)
    return (y * g.astype(jnp.float32)).astype(x.dtype)

def layer_norm(x, g, b):
    xf = x.astype(jnp.float32)
    mu = jnp.mean(xf, axis=-1, keepdims=True)
    xc = xf - mu
    y = xc * lax.rsqrt(jnp.mean(xc * xc, axis=-1, keepdims=True) + EPS)
    return (y * g.astype(jnp.float32) + b.astype(jnp.float32)).astype(x.dtype)

def apply_rope(x, pos):
    half = QK_ROPE // 2
    inv = ROPE_THETA ** (-jnp.arange(half, dtype=jnp.float32) / half)
    ang = pos.astype(jnp.float32)[:, None] * inv[None, :]
    cos = jnp.cos(ang)[:, None, :]
    sin = jnp.sin(ang)[:, None, :]
    xf = x.astype(jnp.float32)
    x1, x2 = xf[..., :half], xf[..., half:]
    return jnp.concatenate([x1 * cos - x2 * sin, x1 * sin + x2 * cos], axis=-1).astype(x.dtype)

def split_in(p):
    sizes = (Q_LORA, KV_LORA, QK_ROPE, 2 * C_CONV, MEM_W, N_BRANCH * D_MODEL)
    cuts = [sum(sizes[:i]) for i in range(1, len(sizes))]
    return jnp.split(p, cuts, axis=-1)

def glu(a):
    u, g = jnp.split(a, 2, axis=-1)
    return u * jax.nn.sigmoid(g)

def swiglu(x, wg, wu, wd):
    return (jax.nn.silu(x @ wg) * (x @ wu)) @ wd

def mla_queries(q_lat, pos, g_q_lora, w_uq, g_q_mla):
    c_q = rms_norm(q_lat, g_q_lora)
    q = c_q @ w_uq
    q = rms_norm(q.reshape(q.shape[:-1] + (MLA_HEADS, QK_HEAD)), g_q_mla)
    return jnp.concatenate([q[..., :QK_NOPE], apply_rope(q[..., QK_NOPE:], pos)], axis=-1)

def mla_keys(c_kv, k_rope, pos, w_uk, g_k_mla):
    k_nope = jnp.einsum('...lc,chd->...lhd', c_kv, w_uk)
    k_r = jnp.broadcast_to(k_rope[..., None, :], k_nope.shape[:-1] + (QK_ROPE,))
    k = rms_norm(jnp.concatenate([k_nope, k_r], axis=-1), g_k_mla)
    return jnp.concatenate([k[..., :QK_NOPE], apply_rope(k[..., QK_NOPE:], pos)], axis=-1)

def attend_latent(q, k, c_kv, qpos, kpos, w_uv):
    s = jnp.einsum('...qhd,...khd->...hqk', q, k).astype(jnp.float32) * MLA_SCALE
    s = jnp.where(kpos[None, :] <= qpos[:, None], s, -1e30)
    p = jax.nn.softmax(s, axis=-1).astype(c_kv.dtype)
    ctx = jnp.einsum('...hqk,...kc->...qhc', p, c_kv)
    return jnp.einsum('...qhc,chv->...qhv', ctx, w_uv)

def mla_prompt(q, k, c_kv, w_uv):
    b, s = q.shape[:2]
    n_qb = s // Q_BLOCK
    kpos = jnp.arange(s)
    qb = q.reshape(b, n_qb, Q_BLOCK, MLA_HEADS, QK_HEAD).swapaxes(0, 1)

    def q_block(args):
        q_i, i = args
        qpos = i * Q_BLOCK + jnp.arange(Q_BLOCK)
        return attend_latent(q_i, k, c_kv, qpos, kpos, w_uv)

    o = lax.map(q_block, (qb, jnp.arange(n_qb)))
    return o.swapaxes(0, 1).reshape(b, s, MLA_HEADS * V_HEAD)

def mla_sample(q, c_new, kr_new, cache_latent, cache_krope, layer, page_table, w_uk, g_k_mla, w_uv):
    db, ds = q.shape[:2]
    past_len = page_table.shape[1] * cache_latent.shape[2]
    qpos = past_len + jnp.arange(ds)
    kpos = jnp.arange(past_len + ds)

    def one_seq(args):
        q_b, pt, c_b, kr_b = args
        c_all = jnp.concatenate([cache_latent[layer, pt].reshape(past_len, KV_LORA), c_b], axis=0)
        kr_all = jnp.concatenate([cache_krope[layer, pt].reshape(past_len, QK_ROPE), kr_b], axis=0)
        k = mla_keys(c_all, kr_all, kpos, w_uk, g_k_mla)
        return attend_latent(q_b, k, c_all, qpos, kpos, w_uv)

    o = lax.map(one_seq, (q, page_table, c_new, kr_new))
    return o.reshape(db, ds, MLA_HEADS * V_HEAD)

def conv_branch(hist, w_dw, b_dw, g_ln, b_ln, w_conv_out):
    y = lax.conv_general_dilated(hist, w_dw[:, None, :], window_strides=(1,), padding='VALID',
                                 dimension_numbers=('NWC', 'WIO', 'NWC'), feature_group_count=C_CONV)
    y = jax.nn.silu(layer_norm(y + b_dw, g_ln, b_ln))
    return y @ w_conv_out

def mem_kv(mem, g_mem_norm, w_mem_kv, g_k_mem):
    m = rms_norm(mem, g_mem_norm) @ w_mem_kv
    k, v = jnp.split(m, 2, axis=-1)
    k = rms_norm(k.reshape(k.shape[:-1] + (MEM_HEADS, MEM_HD)), g_k_mem)
    v = v.reshape(v.shape[:-1] + (MEM_HEADS, MEM_HD))
    return k, v

def mem_attend(q_mem, k, v, g_q_mem, w_o_mem):
    n, l = q_mem.shape[:2]
    q = rms_norm(q_mem.reshape(n, l, MEM_HEADS, MEM_HD), g_q_mem)
    s = jnp.einsum('nlhd,nmhd->nhlm', q, k).astype(jnp.float32) * MEM_SCALE
    p = jax.nn.softmax(s, axis=-1).astype(v.dtype)
    o = jnp.einsum('nhlm,nmhd->nlhd', p, v).reshape(n, l, MEM_W)
    return o @ w_o_mem

def merge_branches(gates, y_mla, y_conv, y_mem, w_out):
    g = jax.nn.sigmoid(gates.astype(jnp.float32)).astype(y_mla.dtype)
    g_a, g_b, g_c = jnp.split(g, N_BRANCH, axis=-1)
    return (g_a * y_mla + g_b * y_conv + g_c * y_mem) @ w_out

def moe(xs, w_router, b_router, w_e_gate, w_e_up, w_e_down, w_s_gate, w_s_up, w_s_down):
    n_tok, d = xs.shape
    scores = jax.nn.sigmoid(jnp.dot(xs.astype(jnp.float32), w_router.astype(jnp.float32)))
    _, top_idx = lax.top_k(scores + b_router.astype(jnp.float32), TOP_K)
    top_w = jnp.take_along_axis(scores, top_idx, axis=-1)
    top_w = top_w / jnp.sum(top_w, axis=-1, keepdims=True) * ROUTED_SCALE
    n_assign = n_tok * TOP_K
    flat_e = top_idx.reshape(-1).astype(jnp.int32)
    flat_t = jnp.arange(n_assign, dtype=jnp.int32) // TOP_K
    flat_w = top_w.reshape(-1)
    order = jnp.argsort(flat_e)
    se, st, sw = flat_e[order], flat_t[order], flat_w[order]
    counts = jnp.zeros((N_EXPERTS,), jnp.int32).at[flat_e].add(1)
    start = jnp.cumsum(counts) - counts
    padded = (counts + MOE_BLOCK - 1) // MOE_BLOCK * MOE_BLOCK
    pend = jnp.cumsum(padded)
    pstart = pend - padded
    dest = pstart[se] + jnp.arange(n_assign, dtype=jnp.int32) - start[se]
    n_blocks = (n_assign + MOE_BLOCK - 1) // MOE_BLOCK + N_EXPERTS
    n_slots = n_blocks * MOE_BLOCK
    slot_tok = jnp.full((n_slots,), n_tok, jnp.int32).at[dest].set(st)
    slot_w = jnp.zeros((n_slots,), jnp.float32).at[dest].set(sw)
    block_e = jnp.minimum(jnp.searchsorted(pend, jnp.arange(n_blocks, dtype=jnp.int32) * MOE_BLOCK, side='right'),
                          N_EXPERTS - 1)
    xs_pad = jnp.concatenate([xs, jnp.zeros((1, d), xs.dtype)], axis=0)

    def run_block(args):
        tok, wt, e = args
        xb = xs_pad[tok]
        return swiglu(xb, w_e_gate[e], w_e_up[e], w_e_down[e]) * wt[:, None].astype(xb.dtype)

    out = lax.map(run_block, (slot_tok.reshape(n_blocks, MOE_BLOCK), slot_w.reshape(n_blocks, MOE_BLOCK), block_e))
    routed = jax.ops.segment_sum(out.reshape(n_slots, d), slot_tok, num_segments=n_tok + 1)[:n_tok]
    return routed + swiglu(xs, w_s_gate, w_s_up, w_s_down)

def channel_mixer(x, g_ffn_norm, w_router, b_router, w_e_gate, w_e_up, w_e_down, w_s_gate, w_s_up, w_s_down):
    shape = x.shape
    h = rms_norm(x, g_ffn_norm).reshape(-1, shape[-1])
    return x + moe(h, w_router, b_router, w_e_gate, w_e_up, w_e_down, w_s_gate, w_s_up, w_s_down).reshape(shape)

def setup_inputs(seed: int = 0) -> dict:
    key = jax.random.key(seed)
    ks = list(jax.random.split(key, 48))
    cnt = [0]

    def nxt():
        cnt[0] += 1
        return ks[cnt[0] - 1]

    def nrm(shape, scale):
        return jax.random.normal(nxt(), shape, jnp.float32) * scale

    def gain(shape):
        return 1.0 + nrm(shape, 0.05)

    n_pages = PAST_LEN // PAGE_SIZE
    n_used = DEC_BATCH * n_pages
    n_phys = n_used + (n_used + 3) // 4
    d, L = D_MODEL, DEPTH
    x_prompt = nrm((BATCH, SEQ, d), 1.0)
    x_sample = nrm((DEC_BATCH, DEC_SEQ, d), 1.0)
    mem_prompt = nrm((BATCH, MEM_TOKENS, d), 1.0)
    cache_latent = nrm((L, n_phys, PAGE_SIZE, KV_LORA), 1.0)
    cache_krope = nrm((L, n_phys, PAGE_SIZE, QK_ROPE), 1.0)
    state_conv = nrm((L, DEC_BATCH, CONV_W - 1, C_CONV), 0.5)
    cache_mem_k = nrm((L, DEC_BATCH, MEM_TOKENS, MEM_HEADS, MEM_HD), 1.0)
    cache_mem_v = nrm((L, DEC_BATCH, MEM_TOKENS, MEM_HEADS, MEM_HD), 1.0)
    page_table = jax.random.permutation(nxt(), n_phys)[:n_used].reshape(DEC_BATCH, n_pages).astype(jnp.int32)
    return {
        'x_prompt': x_prompt, 'x_sample': x_sample, 'mem_prompt': mem_prompt,
        'cache_latent': cache_latent, 'cache_krope': cache_krope, 'state_conv': state_conv,
        'cache_mem_k': cache_mem_k, 'cache_mem_v': cache_mem_v, 'page_table': page_table,
        'g_attn_norm': gain((L, d)),
        'w_in': nrm((L, d, IN_COLS), d ** -0.5),
        'g_q_lora': gain((L, Q_LORA)),
        'w_uq': nrm((L, Q_LORA, MLA_HEADS * QK_HEAD), Q_LORA ** -0.5),
        'g_q_mla': gain((L, QK_HEAD)),
        'g_kv_lora': gain((L, KV_LORA)),
        'w_uk': nrm((L, KV_LORA, MLA_HEADS, QK_NOPE), KV_LORA ** -0.5),
        'w_uv': nrm((L, KV_LORA, MLA_HEADS, V_HEAD), KV_LORA ** -0.5),
        'g_k_mla': gain((L, QK_HEAD)),
        'w_o_mla': nrm((L, MLA_HEADS * V_HEAD, d), (MLA_HEADS * V_HEAD) ** -0.5),
        'w_dw': nrm((L, CONV_W, C_CONV), CONV_W ** -0.5),
        'b_dw': nrm((L, C_CONV), 0.02),
        'g_conv_ln': gain((L, C_CONV)),
        'b_conv_ln': nrm((L, C_CONV), 0.02),
        'w_conv_out': nrm((L, C_CONV, d), C_CONV ** -0.5),
        'g_mem_norm': gain((L, d)),
        'w_mem_kv': nrm((L, d, 2 * MEM_W), d ** -0.5),
        'g_q_mem': gain((L, MEM_HD)),
        'g_k_mem': gain((L, MEM_HD)),
        'w_o_mem': nrm((L, MEM_W, d), MEM_W ** -0.5),
        'w_out': nrm((L, d, d), d ** -0.5),
        'g_ffn_norm': gain((L, d)),
        'w_router': nrm((L, d, N_EXPERTS), d ** -0.5),
        'b_router': nrm((L, N_EXPERTS), 0.01),
        'w_e_gate': nrm((L, N_EXPERTS, d, D_EXPERT), d ** -0.5),
        'w_e_up': nrm((L, N_EXPERTS, d, D_EXPERT), d ** -0.5),
        'w_e_down': nrm((L, N_EXPERTS, D_EXPERT, d), D_EXPERT ** -0.5),
        'w_s_gate': nrm((L, d, D_SHARED), d ** -0.5),
        'w_s_up': nrm((L, d, D_SHARED), d ** -0.5),
        'w_s_down': nrm((L, D_SHARED, d), D_SHARED ** -0.5),
    }

def reference(x_prompt, x_sample, mem_prompt, cache_latent, cache_krope, state_conv, cache_mem_k, cache_mem_v,
              page_table, g_attn_norm, w_in, g_q_lora, w_uq, g_q_mla, g_kv_lora, w_uk, w_uv, g_k_mla, w_o_mla,
              w_dw, b_dw, g_conv_ln, b_conv_ln, w_conv_out, g_mem_norm, w_mem_kv, g_q_mem, g_k_mem, w_o_mem,
              w_out, g_ffn_norm, w_router, b_router, w_e_gate, w_e_up, w_e_down, w_s_gate, w_s_up, w_s_down):
    b, s, _ = x_prompt.shape
    db, ds, _ = x_sample.shape
    past_len = page_table.shape[1] * cache_latent.shape[2]
    pos_p = jnp.arange(s)
    pos_s = past_len + jnp.arange(ds)
    xp, xs = x_prompt, x_sample
    lat_p, kr_p_all, conv_p_all, mk_p_all, mv_p_all = [], [], [], [], []
    lat_s, kr_s_all, conv_s_all = [], [], []
    for l in range(DEPTH):
        hp = rms_norm(xp, g_attn_norm[l])
        q_lat, kv_lat, kr_p, conv_in, qm_p, gt_p = split_in(hp @ w_in[l])
        c_p = rms_norm(kv_lat, g_kv_lora[l])
        q_p = mla_queries(q_lat, pos_p, g_q_lora[l], w_uq[l], g_q_mla[l])
        k_p = mla_keys(c_p, kr_p, pos_p, w_uk[l], g_k_mla[l])
        y_mla_p = mla_prompt(q_p, k_p, c_p, w_uv[l]) @ w_o_mla[l]
        u_p = glu(conv_in)
        hist_p = jnp.concatenate([jnp.zeros((b, CONV_W - 1, C_CONV), u_p.dtype), u_p], axis=1)
        y_conv_p = conv_branch(hist_p, w_dw[l], b_dw[l], g_conv_ln[l], b_conv_ln[l], w_conv_out[l])
        mk_p, mv_p = mem_kv(mem_prompt, g_mem_norm[l], w_mem_kv[l], g_k_mem[l])
        y_mem_p = mem_attend(qm_p, mk_p, mv_p, g_q_mem[l], w_o_mem[l])
        xp = xp + merge_branches(gt_p, y_mla_p, y_conv_p, y_mem_p, w_out[l])
        xp = channel_mixer(xp, g_ffn_norm[l], w_router[l], b_router[l], w_e_gate[l], w_e_up[l], w_e_down[l],
                           w_s_gate[l], w_s_up[l], w_s_down[l])
        lat_p.append(c_p)
        kr_p_all.append(kr_p)
        conv_p_all.append(hist_p[:, -(CONV_W - 1):])
        mk_p_all.append(mk_p)
        mv_p_all.append(mv_p)
        hs = rms_norm(xs, g_attn_norm[l])
        q_lat_s, kv_lat_s, kr_s, conv_in_s, qm_s, gt_s = split_in(hs @ w_in[l])
        c_s = rms_norm(kv_lat_s, g_kv_lora[l])
        q_s = mla_queries(q_lat_s, pos_s, g_q_lora[l], w_uq[l], g_q_mla[l])
        y_mla_s = mla_sample(q_s, c_s, kr_s, cache_latent, cache_krope, l, page_table,
                             w_uk[l], g_k_mla[l], w_uv[l]) @ w_o_mla[l]
        hist_s = jnp.concatenate([state_conv[l], glu(conv_in_s)], axis=1)
        y_conv_s = conv_branch(hist_s, w_dw[l], b_dw[l], g_conv_ln[l], b_conv_ln[l], w_conv_out[l])
        y_mem_s = mem_attend(qm_s, cache_mem_k[l], cache_mem_v[l], g_q_mem[l], w_o_mem[l])
        xs = xs + merge_branches(gt_s, y_mla_s, y_conv_s, y_mem_s, w_out[l])
        xs = channel_mixer(xs, g_ffn_norm[l], w_router[l], b_router[l], w_e_gate[l], w_e_up[l], w_e_down[l],
                           w_s_gate[l], w_s_up[l], w_s_down[l])
        lat_s.append(c_s)
        kr_s_all.append(kr_s)
        conv_s_all.append(hist_s[:, -(CONV_W - 1):])
    return (xp, xs, jnp.stack(lat_p), jnp.stack(kr_p_all), jnp.stack(conv_p_all), jnp.stack(mk_p_all),
            jnp.stack(mv_p_all), jnp.stack(lat_s), jnp.stack(kr_s_all), jnp.stack(conv_s_all))


_drawn_inputs = setup_inputs


def setup_inputs(seed=0):
    import zlib

    import numpy as np

    out = dict(_drawn_inputs(seed))
    spreads = {}
    factors = {'g_q_lora': 2.788, 'g_q_mla': 2.954, 'g_q_mem': 2.875}
    for name, (base, spread) in spreads.items():
        noise = np.random.default_rng([zlib.crc32(name.encode()), seed]).standard_normal(out[name].shape)
        drawn = base * np.exp(spread * noise) if base else spread * noise
        out[name] = __import__('jax').numpy.asarray(drawn.astype(out[name].dtype))
    for name, factor in factors.items():
        out[name] = (out[name] * factor).astype(out[name].dtype)
    return out
```

```python
from contextlib import ExitStack

import numpy as np

import concourse.bass as bass
from concourse import mybir

F32 = mybir.dt.float32
BF16 = mybir.dt.bfloat16
I32 = mybir.dt.int32
ALU = mybir.AluOpType
ACT = mybir.ActivationFunctionType
AX = mybir.AxisListType

P = 128
D = 1024
KD = D // P
SEQ = 1024
NT = SEQ // P
DB = 8
TOK = SEQ + DB
NHEAD, NOPE, ROPE, VH = 8, 64, 32, 64
QH = NOPE + ROPE
LORA = 256
KL = LORA // P
CC = 512
KC = CC // P
CW = 31
HIST = CW - 1
MT = 256
MH, MHD = 4, 128
MW = MH * MHD
PAST = 2048
PAGE = 128
NPAGE = PAST // PAGE
NPHYS = DB * NPAGE + (DB * NPAGE + 3) // 4
NE, TOPK, DE = 64, 8, 256
C_KR = 2 * LORA
C_CONV = C_KR + ROPE
C_QM = C_CONV + 2 * CC
C_GATE = C_QM + MW
EPS = 1e-6
SC_MLA = QH ** -0.5
SC_MEM = MHD ** -0.5


def spread(ap, n, at=1):
    v = ap.unsqueeze(at)
    shape = list(v.shape)
    shape[at] = n
    return v.broadcast_to(shape)


class Core:

    def __init__(self, nc):
        self.nc = nc
        self.stack = ExitStack()
        self.sems = []

    def __enter__(self):
        self.stack.__enter__()
        return self

    def __exit__(self, *a):
        if self.sems and a[0] is None:
            self.nc.clear_and_free_semaphores(self.sems)
            self.nc.all_engine_barrier()
        return self.stack.__exit__(*a)

    def sb(self, name, shape, dt=F32):
        return self.stack.enter_context(self.nc.sbuf_tensor(name, shape, dt))

    def ps(self, name, cols=512, dt=F32):
        return self.stack.enter_context(self.nc.psum_tensor(name, [P, cols], dt))

    def sem(self, name):
        self.sems.append(self.nc.alloc_semaphore(name))
        return self.sems[-1]

    def start_at_one(self, engine, sems, names):
        for name in names.split():
            engine.sem_inc(sems[name], 1)

    def block(self):
        return self.nc.Block()


def stage_constants(nc, a, keep):
    with Core(nc) as c:
        loaded = c.sem("constants_loaded")
        cleared = c.sem("buffers_cleared")
        with c.block() as block:
            @block.sync
            def _(sp):
                sp.dma_start(keep.ident[:, :], a["k_ident"]).then_inc(loaded, 16)
                sp.dma_start(keep.cos[:, :, :], a["k_cos"].rearrange("(t p) c -> p t c", p=P)).then_inc(loaded, 16)
                sp.dma_start(keep.sin[:, :, :], a["k_sin"].rearrange("(t p) c -> p t c", p=P)).then_inc(loaded, 16)
                sp.wait_ge(loaded, 48)

            @block.gpsimd
            def _(pool):
                pool.memset(keep.mhalf[:, :], -0.5).then_inc(cleared, 1)
                pool.wait_ge(cleared, 1)


def stage_memory(nc, a, o, keep):
    W2 = 2 * MW
    with Core(nc) as c:
        w = c.sb("w_mem", [P, KD, W2])
        x = c.sb("mem_x", [P, 2, D])
        h = c.sb("mem_h", [P, D])
        hT = c.sb("mem_hT", [P, KD, P])
        g = c.sb("mem_g", [P, KD])
        gk = c.sb("mem_gk", [P, MHD])
        junk = c.sb("mem_junk", [P, D])
        ss = c.sb("mem_ss", [P, 8])
        rs = c.sb("mem_rs", [P, 8])
        k = c.sb("mem_k", [P, MW])
        kn = c.sb("mem_kn", [P, MH, MHD])
        pT = c.ps("mem_pT", 1024)
        pK = c.ps("mem_pK")
        pV = c.ps("mem_pV")
        x_in, w_in, g_in = c.sem("mem_x_in"), c.sem("mem_w_in"), c.sem("mem_g_in")
        squares, mean, rsq = c.sem("mem_squares"), c.sem("mem_mean"), c.sem("mem_rsq")
        h_ready, hT_psum, hT_ready, kv_psum = c.sem("mem_h_ready"), c.sem("mem_hT_psum"), c.sem("mem_hT_ready"), c.sem("mem_kv_psum")
        v_ready, k_scaled, k_ready, kT_psum, kT_ready, stored = (c.sem(n) for n in (
            "mem_v_ready", "mem_k_scaled", "mem_k_ready", "mem_kT_psum", "mem_kT_ready", "mem_stored"))
        with c.block() as block:
            @block.sync
            def _(sp):
                sp.dma_start(x[:, :, :], a["mem_prompt"][0].rearrange("(t p) d -> p t d", p=P)).then_inc(x_in, 16)
                sp.dma_start(g[:, :], a["g_mem_norm"][0].rearrange("(k p) -> p k", p=P), allow_slow_non_contiguous=True).then_inc(g_in, 16)
                sp.dma_start(gk[:, :], a["g_k_mem"][0].partition_broadcast(P)).then_inc(g_in, 16)
                sp.dma_start(w[:, :, :], a["w_mem_kv"][0].rearrange("(k p) n -> p k n", p=P)).then_inc(w_in, 16)
                for t in range(2):
                    sp.wait_ge(v_ready, t + 1)
                    sp.dma_start(o["mem_v"][t * P:(t + 1) * P, :], keep.mv[:, t, :]).then_inc(stored, 16)
                    sp.wait_ge(k_ready, t + 1)
                    sp.dma_start(o["mem_k"][t * P:(t + 1) * P, :], kn[:, :, :].rearrange("p h d -> p (h d)")).then_inc(stored, 16)
                    sp.wait_ge(stored, 32 * (t + 1))

            @block.scalar
            def _(act):
                act.wait_ge(x_in, 16)
                for t in range(2):
                    act.activation(junk[:, :], x[:, t, :], ACT.Square, accum_out=ss[:, t:t + 1]).then_inc(squares, 1)
                    act.wait_ge(kv_psum, 2 * t + 2)
                    act.activation(k[:, :], pK[:, :], ACT.Copy).then_inc(squares, 1)
                    act.activation(keep.mv[:, t, :], pV[:, :], ACT.Copy).then_inc(v_ready, 1)
                    act.wait_ge(kT_psum, t + 1)
                    act.activation(keep.mkT[:, :, t * P:(t + 1) * P], pT[:, 0:MW].rearrange("p (h n) -> p h n", h=MH),
                                   ACT.Copy).then_inc(kT_ready, 1)

            @block.gpsimd
            def _(pool):
                for t in range(2):
                    pool.wait_ge(mean, 2 * t + 1)
                    pool.tensor_tensor(rs[:, 0:1], ss[:, 2:3], keep.mhalf[:, 0:1], ALU.pow).then_inc(rsq, 1)
                    pool.wait_ge(mean, 2 * t + 2)
                    pool.tensor_tensor(rs[:, 4:8], ss[:, 4:8], keep.mhalf[:, 0:MH], ALU.pow).then_inc(rsq, 1)

            @block.vector
            def _(v):
                v.wait_ge(g_in, 32)
                for t in range(2):
                    v.wait_ge(squares, 2 * t + 1)
                    v.tensor_scalar(ss[:, 2:3], ss[:, t:t + 1], 1.0 / D, EPS, ALU.mult, ALU.add).then_inc(mean, 1)
                    v.wait_ge(rsq, 2 * t + 1)
                    v.tensor_scalar(h[:, :], x[:, t, :], rs[:, 0:1], None, ALU.mult).then_inc(h_ready, 1)
                    v.wait_ge(hT_psum, t + 1)
                    v.tensor_tensor(hT[:, :, :], pT[:, :].rearrange("p (k n) -> p k n", k=KD), spread(g[:, :], P, 2), ALU.mult).then_inc(hT_ready, 1)
                    v.wait_ge(squares, 2 * t + 2)
                    v.tensor_tensor(junk[:, 0:MW], k[:, :], k[:, :], ALU.mult).then_inc(k_scaled, 1)
                    v.wait_ge(k_scaled, 4 * t + 1)
                    v.tensor_reduce(rs[:, 4:8], junk[:, 0:MW].rearrange("p (h d) -> p h d", h=MH), AX.X, ALU.add).then_inc(k_scaled, 1)
                    v.wait_ge(k_scaled, 4 * t + 2)
                    v.tensor_scalar(ss[:, 4:8], rs[:, 4:8], 1.0 / MHD, EPS, ALU.mult, ALU.add).then_inc(mean, 1)
                    v.wait_ge(rsq, 2 * t + 2)
                    v.wait_ge(stored, 32 * t)
                    v.tensor_tensor(junk[:, 0:MW].rearrange("p (h d) -> p h d", h=MH), k[:, :].rearrange("p (h d) -> p h d", h=MH),
                                    spread(rs[:, 4:8], MHD, 2), ALU.mult).then_inc(k_scaled, 1)
                    v.wait_ge(k_scaled, 4 * t + 3)
                    v.tensor_tensor(kn[:, :, :], junk[:, 0:MW].rearrange("p (h d) -> p h d", h=MH), spread(gk[:, :], MH), ALU.mult).then_inc(k_ready, 1)
                    v.sem_inc(k_scaled, 1)

            @block.tensor
            def _(pe):
                for t in range(2):
                    pe.wait_ge(h_ready, t + 1)
                    pe.wait_ge(kT_ready, t)
                    for i in range(KD):
                        mm = pe.transpose(pT[:, i * P:(i + 1) * P], h[:, i * P:(i + 1) * P], keep.ident[:, :])
                    mm.then_inc(hT_psum, 1)
                    pe.wait_ge(hT_ready, t + 1)
                    pe.wait_ge(w_in, 16)
                    pe.wait_ge(v_ready, t)
                    for i in range(KD):
                        mm = pe.matmul(pK[:, :], hT[:, i, :], w[:, i, 0:MW], start=i == 0, stop=i == KD - 1)
                    mm.then_inc(kv_psum, 1)
                    for i in range(KD):
                        mm = pe.matmul(pV[:, :], hT[:, i, :], w[:, i, MW:W2], start=i == 0, stop=i == KD - 1)
                    mm.then_inc(kv_psum, 1)
                    pe.wait_ge(k_ready, t + 1)
                    for i in range(MH):
                        mm = pe.transpose(pT[:, i * P:(i + 1) * P], kn[:, i, :], keep.ident[:, :])
                    mm.then_inc(kT_psum, 1)


class Steps:

    def __init__(self, sem, t, per):
        self.sem, self.base, self.per, self.n = sem, t * per, per, 0

    def mark(self, instruction):
        instruction.then_inc(self.sem, 1)
        self.n += 1

    def wait(self, engine):
        engine.wait_ge(self.sem, self.base + self.n)

    def end(self):
        assert self.n == self.per, (self.n, self.per)


def heads(ap, n):
    return ap.rearrange("p (h d) -> p h d", h=n)


def stage_tokens(nc, a, o, keep):
    C2 = C_CONV
    SM = 16
    with Core(nc) as c:
        w_lat = c.sb("w_lat", [P, KD, C2])
        w_qm = c.sb("w_qm", [P, KD, MW])
        w_uq = c.sb("w_uq", [P, KL, NHEAD * QH])
        w_uk = c.sb("w_uk", [P, KL, NHEAD * NOPE])
        w_uv = c.sb("w_uv", [P, KL, NHEAD * VH])
        g_attn = c.sb("g_attn", [P, KD])
        g_ql = c.sb("g_ql", [P, LORA])
        g_kvl = c.sb("g_kvl", [P, LORA])
        g_q = c.sb("g_q", [P, QH])
        g_k = c.sb("g_k", [P, QH])
        g_qm = c.sb("g_qm", [P, MHD])
        x = c.sb("x", [P, D])
        h = c.sb("h", [P, D])
        hT = c.sb("hT_tile", [P, KD, P])
        junk, sqm = h[:, 0:MW], h[:, MW:2 * MW]
        cq = c.sb("cq", [P, LORA])
        cT = c.sb("cT", [P, KL + KL + MH, P])
        kr_g = c.sb("kr_g", [P, ROPE])
        kr_sq = c.sb("kr_sq", [P, ROPE])
        kr_c = c.sb("kr_c", [P, ROPE])
        kr_s = c.sb("kr_s", [P, ROPE])
        kr_r = c.sb("kr_r", [P, ROPE])
        q_c = c.sb("q_c", [P, NHEAD, ROPE])
        q_s = c.sb("q_s", [P, NHEAD, ROPE])
        qT = c.sb("qT", [QH, NHEAD, P])
        kT = keep.mergedT[0:QH, :, 0:SEQ]
        V = c.sb("V", [P, NT, NHEAD * VH])
        mask = c.sb("mask", [P, SEQ])
        Sm = c.sb("Sm", [P, 2, SEQ])
        PT = c.sb("PT", [P, 2, NT, P])
        flat = Sm[:, :, :].rearrange("p b n -> p (b n)")
        sqq, sqk = heads(flat[:, 0:NHEAD * QH], NHEAD), heads(flat[:, NHEAD * QH:NHEAD * (QH + NOPE)], NHEAD)
        mP = heads(Sm[:, 0, :], MH)
        mPT = PT[:, 0, :, :]
        ob, mob = Sm[:, 1, 0:512], Sm[:, 1, 512:1024]
        oT = c.sb("oT_tile", [P, 2, 4 * P])
        ss = c.sb("ss", [P, 8])
        n1 = c.sb("n1", [P, 8])
        r1 = c.sb("r1", [P, 8])
        n2 = c.sb("n2", [P, SM])
        r2 = c.sb("r2", [P, SM])
        mx = c.sb("mx", [P, SM])
        nb = c.sb("nb", [P, SM])
        ls = c.sb("ls", [P, SM])
        rl = c.sb("rl", [P, SM])
        pT = c.ps("pT", 1024)
        pS = [c.ps("pS0", 1024), c.ps("pS1", 1024)]
        pO = c.ps("pO", 1024)
        pA, pC, pK, pV = pS[0][:, 0:512], pS[0][:, 512:1024], pS[1][:, 0:512], pS[1][:, 512:1024]
        pKR = pK[:, 0:ROPE]
        pQ = pO[:, 0:NHEAD * QH]
        pMO = pO[:, 512:1024]
        pMS = pS[1][:, :]
        qn, kn, ckv, kr, qmn = keep.qn, keep.kn, keep.ckv, keep.kr, keep.qmn
        qn3, kn3 = heads(qn[:, :], NHEAD), heads(kn[:, :], NHEAD)

        names = """w_in gains_in x_in mask_in x_cleared kv_cleared stored h_ready hT_psum hT_ready hT_kept proj_psum
            lat_squares kr_ready c_ready cT_psum cT_ready qkv_psum qkv_squares v_ready qk_ready qT_psum qT_ready kT_psum
            kT_ready s_psum s_masked bias_ready p_ready pt_psum pt_act pt_vec pv_psum o_ready oT_psum oT_ready ms_psum
            m_bias mp_ready mpt_psum mpt_ready mpv_psum mo_ready moT_psum moT_ready x_squares rsq means vsteps a_max a_recip passed passed_sp o_stored""".split()
        S = {n: c.sem("t_" + n) for n in names}

        VS = 16
        with c.block() as block:
            @block.sync
            def _(sp):
                sp.dma_start(g_attn[:, :], a["g_attn_norm"][0].rearrange("(k p) -> p k", p=P), allow_slow_non_contiguous=True).then_inc(S["gains_in"], 16)
                for dst, name in ((g_ql, "g_q_lora"), (g_kvl, "g_kv_lora"), (g_q, "g_q_mla"), (g_k, "g_k_mla"), (g_qm, "g_q_mem")):
                    sp.dma_start(dst[:, :], a[name][0].partition_broadcast(P)).then_inc(S["gains_in"], 16)
                w = a["w_in"][0].rearrange("(k p) n -> p k n", p=P)
                sp.dma_start(w_lat[:, :, :], w[:, :, 0:C2]).then_inc(S["w_in"], 16)
                sp.dma_start(w_qm[:, :, :], w[:, :, C_QM:C_QM + MW]).then_inc(S["w_in"], 16)
                sp.dma_start(w_uq[:, :, :], a["w_uq"][0].rearrange("(k p) n -> p k n", p=P)).then_inc(S["w_in"], 16)
                sp.dma_start(w_uk[:, :, :], a["w_uk"][0].rearrange("(k p) h n -> p k (h n)", p=P)).then_inc(S["w_in"], 16)
                sp.dma_start(w_uv[:, :, :], a["w_uv"][0].rearrange("(k p) h n -> p k (h n)", p=P)).then_inc(S["w_in"], 16)

                def tile(t):
                    sp.wait_ge(S["h_ready"], 1 + t)
                    sp.dma_start(x[:, :], a["x_prompt"][0][bass.ds(t * P, P), :]).then_inc(S["x_in"], 16)
                    sp.wait_ge(S["s_masked"], 1 + NHEAD * t)
                    sp.dma_start(mask[:, :], a["k_mask"][bass.ds(t * P, P), :]).then_inc(S["mask_in"], 16)
                    sp.wait_ge(S["c_ready"], t + 1)
                    sp.dma_start(o["lat_p"][bass.ds(t * P, P), :], ckv[:, :]).then_inc(S["stored"], 16)
                    sp.wait_ge(S["stored"], 1 + 32 * t + 16)
                    sp.dma_start(o["kr_p"][bass.ds(t * P, P), :], kr[:, :]).then_inc(S["stored"], 16)
                    sp.wait_ge(S["stored"], 1 + 32 * t + 32)
                    sp.sem_inc(S["passed_sp"], 1)

                with sp.Fori(0, NT) as t:
                    tile(t)
                sp.wait_ge(S["x_cleared"], 1)
                sp.dma_start(x[0:DB, :], a["x_sample"].rearrange("b s d -> (b s) d")).then_inc(S["x_in"], 16)
                sp.wait_ge(S["c_ready"], NT + 1)
                sp.dma_start(o["lat_s"], ckv[0:DB, :]).then_inc(S["stored"], 16)
                sp.dma_start(o["kr_s"], kr[0:DB, :]).then_inc(S["stored"], 16)
                sp.wait_ge(S["stored"], 1 + 32 * NT + 32)

            @block.gpsimd
            def _(pool):
                pool.memset(kT, 0.0).then_inc(S["kv_cleared"], 1)
                pool.memset(V[:, :, :], 0.0).then_inc(S["kv_cleared"], 1)

                def tile(t, at, cols):
                    pool.wait_ge(S["means"], 3 * t + 1)
                    pool.tensor_tensor(r1[:, 0:1], n1[:, 0:1], keep.mhalf[:, 0:1], ALU.pow).then_inc(S["rsq"], 1)
                    pool.wait_ge(S["hT_ready"], t + 1)
                    pool.tensor_copy(keep.hT[:, :, at], hT[:, :, 0:cols]).then_inc(S["hT_kept"], 1)
                    pool.wait_ge(S["means"], 3 * t + 2)
                    pool.tensor_tensor(r1[:, 1:7], n1[:, 1:7], keep.mhalf[:, 1:7], ALU.pow).then_inc(S["rsq"], 1)
                    pool.wait_ge(S["means"], 3 * t + 3)
                    pool.tensor_tensor(r2[:, :], n2[:, :], keep.mhalf[:, 0:SM], ALU.pow).then_inc(S["rsq"], 1)

                with pool.Fori(0, NT) as t:
                    tile(t, bass.ds(t * P, P), P)
                tile(NT, slice(SEQ, TOK), DB)

            @block.scalar
            def _(act):
                c.start_at_one(act, S, "h_ready s_masked stored o_stored hT_psum hT_kept moT_ready")
                def front(t, x_count, v_at):
                    act.wait_ge(S["x_in"], x_count)
                    act.activation(h[:, :], x[:, :], ACT.Square, accum_out=ss[:, 0:1]).then_inc(S["x_squares"], 1)
                    act.wait_ge(S["proj_psum"], t + 1)
                    act.wait_ge(S["stored"], 1 + 32 * t)
                    act.activation(kr[:, :], pKR, ACT.Copy).then_inc(S["kr_ready"], 1)
                    act.activation(junk[:, 0:LORA], pA[:, 0:LORA], ACT.Square, accum_out=ss[:, 1:2])
                    act.activation(junk[:, LORA:2 * LORA], pA[:, LORA:2 * LORA], ACT.Square, accum_out=ss[:, 2:3])
                    act.activation(kr_sq[:, :], pKR, ACT.Square, accum_out=ss[:, 3:4])
                    act.activation(sqm, pC, ACT.Square).then_inc(S["lat_squares"], 1)
                    act.wait_ge(S["cT_psum"], t + 1)
                    act.activation(cT[:, :, :], pT[:, :].rearrange("p (k n) -> p k n", k=KD), ACT.Copy).then_inc(S["cT_ready"], 1)
                    act.wait_ge(S["qkv_psum"], t + 1)
                    act.activation(sqq, heads(pQ, NHEAD), ACT.Square)
                    act.activation(sqk, heads(pK, NHEAD), ACT.Square).then_inc(S["qkv_squares"], 1)
                    if v_at is not None:
                        act.activation(v_at, pV, ACT.Copy).then_inc(S["v_ready"], 1)

                def attention(t, nk):
                    act.wait_ge(S["qT_psum"], t + 1)
                    act.activation(qT[:, :, :], heads(pT[0:QH, :], NHEAD), ACT.Copy).then_inc(S["qT_ready"], 1)
                    for i in range(NHEAD):
                        b = i % 2
                        act.wait_ge(S["bias_ready"], NHEAD * t + i + 1)
                        act.activation(Sm[:, b, 0:nk * P], Sm[:, b, 0:nk * P], ACT.Exp, bias=nb[:, i:i + 1], scale=SC_MLA,
                                       accum_out=ls[:, i:i + 1]).then_inc(S["p_ready"], 1)
                        act.wait_ge(S["pt_psum"], NHEAD * t + i + 1)
                        if i >= 2:
                            act.wait_ge(S["pv_psum"], NHEAD * t + i - 1)
                        act.activation(PT[:, b, 0:4, :], pT[:, 0:512].rearrange("p (k n) -> p k n", k=4), ACT.Copy).then_inc(S["pt_act"], 1)
                    act.wait_ge(S["m_bias"], t + 1)
                    for i in range(MH):
                        e = act.activation(mP[:, i, :], pMS[:, i * MT:(i + 1) * MT], ACT.Exp, bias=nb[:, NHEAD + i:NHEAD + i + 1],
                                           scale=SC_MEM, accum_out=ls[:, NHEAD + i:NHEAD + i + 1])
                    e.then_inc(S["mp_ready"], 1)
                    act.wait_ge(S["mpt_psum"], t + 1)
                    act.wait_ge(S["pv_psum"], NHEAD * t + NHEAD - 1)
                    act.activation(mPT, pT[:, :].rearrange("p (k n) -> p k n", k=8), ACT.Copy).then_inc(S["mpt_ready"], 1)
                    act.wait_ge(S["oT_psum"], t + 1)
                    act.wait_ge(S["o_stored"], 1 + 16 * t)
                    act.activation(oT[:, 0, :], pT[:, 0:512], ACT.Copy).then_inc(S["oT_ready"], 1)
                    act.wait_ge(S["moT_psum"], t + 1)
                    act.activation(oT[:, 1, :], pT[:, 512:1024], ACT.Copy).then_inc(S["moT_ready"], 1)
                    act.wait_ge(S["moT_ready"], 1 + t + 1)
                    act.dma_start(keep.o_dram[t], oT[:, :, :]).then_inc(S["o_stored"], 16)

                act.wait_ge(S["kv_cleared"], 2)
                for first, last, nk in ((0, NT // 2, NT // 2), (NT // 2, NT, NT)):
                    with act.Fori(first, last) as t:
                        front(t, 16 * t + 16, V[:, t, :])
                        attention(t, nk)
                front(NT, 16 * NT + 16, None)
                act.wait_ge(S["o_stored"], 1 + 16 * NT)

            @block.vector
            def _(v):
                v.wait_ge(S["gains_in"], 96)

                def front(t, cos, sin):
                    own = Steps(S["vsteps"], t, VS)
                    v.wait_ge(S["x_squares"], t + 1)
                    v.tensor_scalar(n1[:, 0:1], ss[:, 0:1], 1.0 / D, EPS, ALU.mult, ALU.add).then_inc(S["means"], 1)
                    v.wait_ge(S["rsq"], 3 * t + 1)
                    v.wait_ge(S["hT_psum"], 1 + t)
                    v.tensor_scalar(h[:, :], x[:, :], r1[:, 0:1], None, ALU.mult).then_inc(S["h_ready"], 1)
                    v.wait_ge(S["hT_psum"], 1 + t + 1)
                    v.wait_ge(S["hT_kept"], 1 + t)
                    v.tensor_tensor(hT[:, :, :], pT[:, :].rearrange("p (k n) -> p k n", k=KD), spread(g_attn[:, :], P, 2), ALU.mult).then_inc(S["hT_ready"], 1)
                    v.wait_ge(S["lat_squares"], t + 1)
                    own.mark(v.tensor_reduce(ss[:, 4:8], heads(sqm, MH), AX.X, ALU.add))
                    v.tensor_scalar(n1[:, 1:3], ss[:, 1:3], 1.0 / LORA, EPS, ALU.mult, ALU.add)
                    own.wait(v)
                    v.tensor_scalar(n1[:, 3:7], ss[:, 4:8], 1.0 / MHD, EPS, ALU.mult, ALU.add).then_inc(S["means"], 1)
                    own.mark(v.tensor_tensor(kr_g[:, :], kr[:, :], g_k[:, NOPE:QH], ALU.mult))
                    own.wait(v)
                    v.tensor_tensor(kr_c[:, :], kr_g[:, :], cos, ALU.mult)
                    own.mark(v.tensor_tensor(kr_s[:, :], kr_g[:, :], sin, ALU.mult))
                    own.wait(v)
                    v.tensor_tensor(kr_r[:, 0:16], kr_c[:, 0:16], kr_s[:, 16:32], ALU.subtract)
                    own.mark(v.tensor_tensor(kr_r[:, 16:32], kr_c[:, 16:32], kr_s[:, 0:16], ALU.add))
                    v.wait_ge(S["rsq"], 3 * t + 2)
                    v.wait_ge(S["stored"], 1 + 32 * t)
                    v.scalar_tensor_tensor(cq[:, :], pA[:, 0:LORA], r1[:, 1:2], g_ql[:, :], ALU.mult, ALU.mult)
                    v.scalar_tensor_tensor(ckv[:, :], pA[:, LORA:2 * LORA], r1[:, 2:3], g_kvl[:, :], ALU.mult, ALU.mult)
                    own.mark(v.tensor_tensor(heads(qmn[:, :], MH), heads(pC, MH), spread(r1[:, 3:7], MHD, 2), ALU.mult))
                    own.wait(v)
                    v.tensor_tensor(heads(qmn[:, :], MH), heads(qmn[:, :], MH), spread(g_qm[:, :], MH), ALU.mult).then_inc(S["c_ready"], 1)
                    v.wait_ge(S["qkv_squares"], t + 1)
                    own.mark(v.tensor_reduce(n2[:, 0:8], sqq, AX.X, ALU.add))
                    own.mark(v.tensor_reduce(n2[:, 8:16], sqk, AX.X, ALU.add))
                    own.wait(v)
                    own.mark(v.tensor_scalar(n2[:, 8:16], n2[:, 8:16], ss[:, 3:4], None, ALU.add))
                    own.wait(v)
                    v.tensor_scalar(n2[:, :], n2[:, :], 1.0 / QH, EPS, ALU.mult, ALU.add).then_inc(S["means"], 1)
                    v.wait_ge(S["rsq"], 3 * t + 3)
                    own.mark(v.tensor_tensor(qn3, heads(pQ, NHEAD), spread(r2[:, 0:8], QH, 2), ALU.mult))
                    own.mark(v.tensor_tensor(kn3[:, :, 0:NOPE], heads(pK, NHEAD), spread(r2[:, 8:16], NOPE, 2), ALU.mult))
                    own.mark(v.tensor_tensor(kn3[:, :, NOPE:QH], spread(kr_r[:, :], NHEAD), spread(r2[:, 8:16], ROPE, 2), ALU.mult))
                    own.wait(v)
                    own.mark(v.tensor_tensor(qn3, qn3, spread(g_q[:, :], NHEAD), ALU.mult))
                    own.mark(v.tensor_tensor(kn3[:, :, 0:NOPE], kn3[:, :, 0:NOPE], spread(g_k[:, 0:NOPE], NHEAD), ALU.mult))
                    own.wait(v)
                    own.mark(v.tensor_tensor(q_c[:, :, :], qn3[:, :, NOPE:QH], spread(cos, NHEAD), ALU.mult))
                    own.mark(v.tensor_tensor(q_s[:, :, :], qn3[:, :, NOPE:QH], spread(sin, NHEAD), ALU.mult))
                    own.wait(v)
                    own.mark(v.tensor_tensor(qn3[:, :, NOPE:NOPE + 16], q_c[:, :, 0:16], q_s[:, :, 16:32], ALU.subtract))
                    v.tensor_tensor(qn3[:, :, NOPE + 16:QH], q_c[:, :, 16:32], q_s[:, :, 0:16], ALU.add).then_inc(S["qk_ready"], 1)
                    own.end()

                def attention(t, nk):
                    v.wait_ge(S["kT_psum"], t + 1)
                    v.tensor_copy(kT[:, :, bass.ds(t * P, P)], heads(pS[0][0:QH, :], NHEAD)).then_inc(S["kT_ready"], 1)
                    v.wait_ge(S["mask_in"], 16 * t + 16)
                    half = nk * P // 2

                    def evacuate(i):
                        if nk == NT:
                            v.wait_ge(S["pt_psum"], NHEAD * t + i + 1)
                            if i >= 2:
                                v.wait_ge(S["pv_psum"], NHEAD * t + i - 1)
                            v.tensor_copy(PT[:, i % 2, 4:8, :], pT[:, 512:1024].rearrange("p (k n) -> p k n", k=4)).then_inc(S["pt_vec"], 1)
                        else:
                            v.sem_inc(S["pt_vec"], 1)

                    for i in range(NHEAD):
                        b = i % 2
                        v.wait_ge(S["s_psum"], NHEAD * t + i + 1)
                        if i >= 2:
                            v.wait_ge(S["pt_psum"], NHEAD * t + i - 1)
                        v.sem_inc(S["passed"], 1)
                        v.tensor_tensor_reduce(Sm[:, b, 0:nk * P], pS[b][:, 0:nk * P], mask[:, 0:nk * P], 1.0, -3.0e38, ALU.add, ALU.max,
                                               mx[:, i:i + 1]).then_inc(S["s_masked"], 1)
                        v.wait_ge(S["s_masked"], 1 + NHEAD * t + i + 1)
                        v.tensor_scalar(nb[:, i:i + 1], mx[:, i:i + 1], -SC_MLA, None, ALU.mult).then_inc(S["bias_ready"], 1)
                        if i >= 1:
                            evacuate(i - 1)
                    evacuate(NHEAD - 1)
                    v.wait_ge(S["ms_psum"], t + 1)
                    v.tensor_reduce(mx[:, 8:12], heads(pMS, MH), AX.X, ALU.max).then_inc(S["a_max"], 1)
                    v.wait_ge(S["a_max"], t + 1)
                    v.tensor_scalar(nb[:, 8:12], mx[:, 8:12], -SC_MEM, None, ALU.mult).then_inc(S["m_bias"], 1)
                    v.wait_ge(S["mp_ready"], t + 1)
                    v.wait_ge(S["pv_psum"], NHEAD * t + NHEAD)
                    v.reciprocal(rl[:, 0:12], ls[:, 0:12]).then_inc(S["a_recip"], 1)
                    v.wait_ge(S["a_recip"], t + 1)
                    v.tensor_tensor(heads(ob, NHEAD), heads(pO[:, 0:512], NHEAD), spread(rl[:, 0:8], VH, 2), ALU.mult).then_inc(S["o_ready"], 1)
                    v.wait_ge(S["mpv_psum"], t + 1)
                    v.tensor_tensor(heads(mob, MH), heads(pMO, MH), spread(rl[:, 8:12], MHD, 2), ALU.mult).then_inc(S["mo_ready"], 1)

                v.wait_ge(S["kv_cleared"], 2)
                for first, last, nk in ((0, NT // 2, NT // 2), (NT // 2, NT, NT)):
                    with v.Fori(first, last) as t:
                        front(t, keep.cos[:, t, :], keep.sin[:, t, :])
                        attention(t, nk)
                v.memset(x[:, :], 0.0).then_inc(S["x_cleared"], 1)
                front(NT, keep.cos[:, NPAGE, :], keep.sin[:, NPAGE, :])

            @block.tensor
            def _(pe):
                def front(t):
                    pe.wait_ge(S["h_ready"], 1 + t + 1)
                    pe.wait_ge(S["moT_ready"], 1 + t)
                    for i in range(KD):
                        mm = pe.transpose(pT[:, i * P:(i + 1) * P], h[:, i * P:(i + 1) * P], keep.ident[:, :])
                    mm.then_inc(S["hT_psum"], 1)
                    pe.wait_ge(S["hT_ready"], t + 1)
                    pe.wait_ge(S["w_in"], 80)
                    for i in range(KD):
                        pe.matmul(pA, hT[:, i, :], w_lat[:, i, 0:C_KR], start=i == 0, stop=i == KD - 1)
                    for i in range(KD):
                        pe.matmul(pKR, hT[:, i, :], w_lat[:, i, C_KR:C_CONV], start=i == 0, stop=i == KD - 1)
                    for i in range(KD):
                        mm = pe.matmul(pC, hT[:, i, :], w_qm[:, i, :], start=i == 0, stop=i == KD - 1)
                    mm.then_inc(S["proj_psum"], 1)
                    pe.wait_ge(S["c_ready"], t + 1)
                    for n, src in enumerate([cq[:, 0:P], cq[:, P:2 * P], ckv[:, 0:P], ckv[:, P:2 * P]] + [qmn[:, i * P:(i + 1) * P] for i in range(MH)]):
                        mm = pe.transpose(pT[:, n * P:(n + 1) * P], src, keep.ident[:, :])
                    mm.then_inc(S["cT_psum"], 1)
                    pe.wait_ge(S["cT_ready"], t + 1)
                    for lo, hi in ((0, 512), (512, NHEAD * QH)):
                        for i in range(KL):
                            pe.matmul(pQ[:, lo:hi], cT[:, i, :], w_uq[:, i, lo:hi], start=i == 0, stop=i == KL - 1)
                    for i in range(KL):
                        pe.matmul(pK, cT[:, KL + i, :], w_uk[:, i, :], start=i == 0, stop=i == KL - 1)
                    for i in range(KL):
                        mm = pe.matmul(pV, cT[:, KL + i, :], w_uv[:, i, :], start=i == 0, stop=i == KL - 1)
                    mm.then_inc(S["qkv_psum"], 1)

                def attention(t, nk):
                    pe.wait_ge(S["qk_ready"], t + 1)
                    for i in range(NHEAD):
                        mm = pe.transpose(pT[0:QH, i * P:(i + 1) * P], qn[:, i * QH:(i + 1) * QH], keep.ident[:, :])
                    mm.then_inc(S["qT_psum"], 1)
                    for i in range(NHEAD):
                        mm = pe.transpose(pS[0][0:QH, i * P:(i + 1) * P], kn[:, i * QH:(i + 1) * QH], keep.ident[:, :])
                    mm.then_inc(S["kT_psum"], 1)
                    pe.wait_ge(S["qT_ready"], t + 1)
                    pe.wait_ge(S["kT_ready"], t + 1)
                    pe.wait_ge(S["v_ready"], t + 1)

                    def scores(i):
                        if i >= 2:
                            pe.wait_ge(S["s_masked"], 1 + NHEAD * t + i - 1)
                        for j in range(0, nk, 4):
                            mm = pe.matmul(pS[i % 2][:, j * P:(j + 4) * P], qT[:, i, :], kT[:, i, j * P:(j + 4) * P], start=True, stop=True)
                        mm.then_inc(S["s_psum"], 1)

                    scores(0)
                    scores(1)
                    for i in range(NHEAD):
                        b = i % 2
                        pe.wait_ge(S["p_ready"], NHEAD * t + i + 1)
                        if i:
                            pe.wait_ge(S["pt_act"], NHEAD * t + i)
                            pe.wait_ge(S["pt_vec"], NHEAD * t + i)
                        for j in range(nk):
                            mm = pe.transpose(pT[:, j * P:(j + 1) * P], Sm[:, b, j * P:(j + 1) * P], keep.ident[:, :])
                        mm.then_inc(S["pt_psum"], 1)
                        if i + 2 < NHEAD:
                            scores(i + 2)
                        pe.wait_ge(S["pt_act"], NHEAD * t + i + 1)
                        pe.wait_ge(S["pt_vec"], NHEAD * t + i + 1)
                        for j in range(nk):
                            mm = pe.matmul(pO[:, i * VH:(i + 1) * VH], PT[:, b, j, :], V[:, j, i * VH:(i + 1) * VH], start=j == 0, stop=j == nk - 1)
                        mm.then_inc(S["pv_psum"], 1)
                    pe.wait_ge(S["s_masked"], 1 + NHEAD * t + NHEAD)
                    for i in range(MH):
                        mm = pe.matmul(pMS[:, i * MT:(i + 1) * MT], cT[:, 2 * KL + i, :], keep.mkT[:, i, :], start=True, stop=True)
                    mm.then_inc(S["ms_psum"], 1)
                    pe.wait_ge(S["mp_ready"], t + 1)
                    for i in range(2 * MH):
                        mm = pe.transpose(pT[:, i * P:(i + 1) * P], mP[:, i // 2, (i % 2) * P:(i % 2 + 1) * P], keep.ident[:, :])
                    mm.then_inc(S["mpt_psum"], 1)
                    pe.wait_ge(S["mpt_ready"], t + 1)
                    for i in range(MH):
                        for j in range(2):
                            mm = pe.matmul(pMO[:, i * MHD:(i + 1) * MHD], mPT[:, 2 * i + j, :], keep.mv[:, j, i * MHD:(i + 1) * MHD], start=j == 0, stop=j == 1)
                    mm.then_inc(S["mpv_psum"], 1)
                    pe.wait_ge(S["o_ready"], t + 1)
                    for i in range(4):
                        mm = pe.transpose(pT[:, i * P:(i + 1) * P], ob[:, i * P:(i + 1) * P], keep.ident[:, :])
                    mm.then_inc(S["oT_psum"], 1)
                    pe.wait_ge(S["mo_ready"], t + 1)
                    for i in range(4):
                        mm = pe.transpose(pT[:, 512 + i * P:512 + (i + 1) * P], mob[:, i * P:(i + 1) * P], keep.ident[:, :])
                    mm.then_inc(S["moT_psum"], 1)

                for first, last, nk in ((0, NT // 2, NT // 2), (NT // 2, NT, NT)):
                    with pe.Fori(first, last) as t:
                        front(t)
                        attention(t, nk)
                front(NT)


def stage_conv(nc, a, o, keep):
    GROUPS = ((0, 512), (512, 512), (SEQ, DB))
    with Core(nc) as c:
        w = c.sb("w_conv", [P, KD, 2 * CC])
        taps = c.sb("taps", [P, KC, CW])
        wrow = c.sb("tap_rows", [CW, CC])
        b_dw = c.sb("b_dw", [P, KC])
        g_ln = c.sb("g_ln", [P, KC])
        b_ln = c.sb("b_ln", [P, KC])
        sig = c.sb("sig", [P, TOK])
        hist = c.sb("hist", [P, KC, HIST + SEQ])
        state = c.sb("state", [120, 2, CC])
        hist_s = c.sb("hist_s", [P, KC, DB, CW])
        prod_s = c.sb("prod_s", [P, DB, CW])
        y = c.sb("y_conv", [P, KC, TOK])
        mean = c.sb("ln_mean", [P, TOK])
        ones = c.sb("ones", [P, P])
        last = c.sb("last_rows", [HIST, CC])
        last_s = c.sb("last_rows_s", [DB, CC])
        eps = c.sb("eps", [P, 1])
        sq = keep.convT
        pU, pG, pM = c.ps("pU", 1024), c.ps("pG", 1024), c.ps("pM", 1024)
        pX, pT = c.ps("pX"), c.ps("pTc")
        S = {n: c.sem("c_" + n) for n in """w_in small_in state_in cleared u_psum sig_ready glu_ready taps_psum taps_ready
            state_psum state_ready tap conv_s mean_psum mean_ready centred squares var_psum sqrt_ready recip normed
            conv_ready last_psum last_ready stored state_moved""".split()}
        with c.block() as block:
            @block.sync
            def _(sp):
                wv = a["w_in"][0].rearrange("(k p) n -> p k n", p=P)
                sp.dma_start(wrow[:, :], a["w_dw"][0]).then_inc(S["small_in"], 16)
                for dst, name in ((b_dw, "b_dw"), (g_ln, "g_conv_ln"), (b_ln, "b_conv_ln")):
                    sp.dma_start(dst[:, :], a[name][0].rearrange("(k p) -> p k", p=P), allow_slow_non_contiguous=True).then_inc(S["small_in"], 16)
                sp.dma_start(state[:, :, :], a["state_conv"][0].rearrange("(g b) r c -> (b r) g c", g=2)).then_inc(S["state_in"], 16)
                sp.dma_start(w[:, :, :], wv[:, :, C_CONV:C_CONV + 2 * CC]).then_inc(S["w_in"], 16)
                sp.dma_start(o["conv_s"][:, 0:HIST - 1, :], a["state_conv"][0][:, 1:HIST, :]).then_inc(S["state_moved"], 16)
                sp.wait_ge(S["last_ready"], 2)
                sp.dma_start(o["conv_p"], last[:, :]).then_inc(S["stored"], 16)
                sp.dma_start(o["conv_s"][:, HIST - 1, :], last_s[:, :]).then_inc(S["stored"], 16)
                sp.wait_ge(S["stored"], 32)
                sp.wait_ge(S["state_moved"], 16)

            @block.gpsimd
            def _(pool):
                pool.memset(ones[:, :], 1.0).then_inc(S["cleared"], 1)
                pool.memset(hist[:, :, 0:HIST], 0.0).then_inc(S["cleared"], 1)
                pool.memset(eps[:, :], EPS).then_inc(S["cleared"], 1)

            @block.scalar
            def _(act):
                act.wait_ge(S["taps_psum"], 1)
                act.activation(taps[:, :, :], pT[:, 0:KC * CW].rearrange("p (k n) -> p k n", k=KC), ACT.Copy).then_inc(S["taps_ready"], 1)
                for g in range(2):
                    act.wait_ge(S["state_psum"], g + 1)
                    act.activation(hist_s[:, :, 4 * g:4 * g + 4, 0:HIST],
                                   pT[:, 0:480].rearrange("p (k b r) -> p k b r", k=KC, b=4), ACT.Copy).then_inc(S["state_ready"], 1)
                for i in range(KC):
                    act.wait_ge(S["u_psum"], i + 1)
                    act.wait_ge(S["glu_ready"], i)
                    act.activation(sig[:, 0:SEQ], pG[:, :], ACT.Sigmoid)
                    act.activation(sig[:, SEQ:TOK], pX[:, DB:2 * DB], ACT.Sigmoid).then_inc(S["sig_ready"], 1)
                act.wait_ge(S["centred"], 1)
                act.activation(sq[:, :, :], y[:, :, :], ACT.Square).then_inc(S["squares"], 1)
                act.wait_ge(S["var_psum"], 1)
                act.activation(mean[:, 0:SEQ], pM[:, :], ACT.Sqrt, scale=1.0 / CC, bias=eps[:, :])
                act.activation(mean[:, SEQ:TOK], pX[:, 16:16 + DB], ACT.Sqrt, scale=1.0 / CC, bias=eps[:, :]).then_inc(S["sqrt_ready"], 1)
                for i in range(KC):
                    act.wait_ge(S["normed"], i + 1)
                    act.activation(keep.convT[:, i, :], y[:, i, :], ACT.Silu, scale=g_ln[:, i:i + 1], bias=b_ln[:, i:i + 1]).then_inc(S["conv_ready"], 1)

            @block.vector
            def _(v):
                v.wait_ge(S["small_in"], 64)
                v.wait_ge(S["taps_ready"], 1)
                v.wait_ge(S["state_ready"], 2)
                v.wait_ge(S["cleared"], 3)
                for i in range(KC):
                    v.wait_ge(S["sig_ready"], i + 1)
                    v.tensor_tensor(hist[:, i, HIST:], pU[:, :], sig[:, 0:SEQ], ALU.mult)
                    v.tensor_tensor(hist_s[:, i, :, HIST], pX[:, 0:DB], sig[:, SEQ:TOK], ALU.mult).then_inc(S["glu_ready"], 1)
                    v.wait_ge(S["glu_ready"], i + 1)
                    v.tensor_scalar(y[:, i, 0:SEQ], hist[:, i, 0:SEQ], taps[:, i, 0:1], b_dw[:, i:i + 1], ALU.mult, ALU.add).then_inc(S["tap"], 1)
                    for j in range(1, CW):
                        v.wait_ge(S["tap"], CW * i + j)
                        v.scalar_tensor_tensor(y[:, i, 0:SEQ], hist[:, i, j:j + SEQ], taps[:, i, j:j + 1], y[:, i, 0:SEQ],
                                               ALU.mult, ALU.add).then_inc(S["tap"], 1)
                    v.tensor_tensor(prod_s[:, :, :], hist_s[:, i, :, :], spread(taps[:, i, :], DB), ALU.mult).then_inc(S["conv_s"], 1)
                    v.wait_ge(S["conv_s"], 3 * i + 1)
                    v.tensor_reduce(y[:, i, SEQ:TOK], prod_s[:, :, :], AX.X, ALU.add).then_inc(S["conv_s"], 1)
                    v.wait_ge(S["conv_s"], 3 * i + 2)
                    v.tensor_scalar(y[:, i, SEQ:TOK], y[:, i, SEQ:TOK], b_dw[:, i:i + 1], None, ALU.add).then_inc(S["conv_s"], 1)
                v.wait_ge(S["mean_psum"], 1)
                v.tensor_scalar(mean[:, 0:SEQ], pM[:, :], -1.0 / CC, None, ALU.mult)
                v.tensor_scalar(mean[:, SEQ:TOK], pX[:, 0:DB], -1.0 / CC, None, ALU.mult).then_inc(S["mean_ready"], 1)
                v.wait_ge(S["mean_ready"], 1)
                v.tensor_tensor(y[:, :, :], y[:, :, :], spread(mean[:, :], KC), ALU.add).then_inc(S["centred"], 1)
                v.wait_ge(S["sqrt_ready"], 1)
                v.reciprocal(mean[:, :], mean[:, :]).then_inc(S["recip"], 1)
                v.wait_ge(S["recip"], 1)
                for i in range(KC):
                    v.tensor_tensor(y[:, i, :], y[:, i, :], mean[:, :], ALU.mult).then_inc(S["normed"], 1)
                v.wait_ge(S["last_psum"], 1)
                v.tensor_copy(last[:, :], pG[0:HIST, 0:CC]).then_inc(S["last_ready"], 1)
                v.tensor_copy(last_s[:, :], pG[0:DB, CC:2 * CC]).then_inc(S["last_ready"], 1)

            @block.tensor
            def _(pe):
                pe.wait_ge(S["small_in"], 64)
                for i in range(KC):
                    mm = pe.transpose(pT[:, i * CW:(i + 1) * CW], wrow[:, i * P:(i + 1) * P], keep.ident[0:CW, 0:CW])
                mm.then_inc(S["taps_psum"], 1)
                pe.wait_ge(S["state_in"], 16)
                pe.wait_ge(S["taps_ready"], 1)
                for g in range(2):
                    pe.wait_ge(S["state_ready"], g)
                    for i in range(KC):
                        mm = pe.transpose(pT[:, i * 120:(i + 1) * 120], state[:, g, i * P:(i + 1) * P], keep.ident[0:120, 0:120])
                    mm.then_inc(S["state_psum"], 1)
                pe.wait_ge(S["w_in"], 16)
                for i in range(KC):
                    pe.wait_ge(S["glu_ready"], i)
                    for dst, base, xcol in ((pU, 0, 0), (pG, CC, DB)):
                        for at, n in GROUPS:
                            out = dst[:, at:at + n] if n == 512 else pX[:, xcol:xcol + n]
                            for k in range(KD):
                                mm = pe.matmul(out, w[:, k, base + i * P:base + (i + 1) * P], keep.hT[:, k, at:at + n], start=k == 0, stop=k == KD - 1)
                    mm.then_inc(S["u_psum"], 1)
                pe.wait_ge(S["conv_s"], 3 * KC)
                pe.wait_ge(S["cleared"], 3)
                for src, done, wait in ((y, "mean_psum", None), (sq, "var_psum", "squares")):
                    if wait:
                        pe.wait_ge(S[wait], 1)
                    for at, n in GROUPS:
                        out = pM[:, at:at + n] if n == 512 else pX[:, (16 if wait else 0):(16 if wait else 0) + n]
                        for i in range(KC):
                            mm = pe.matmul(out, ones[:, :], src[:, i, at:at + n], start=i == 0, stop=i == KC - 1)
                    mm.then_inc(S[done], 1)
                for i in range(KC):
                    pe.transpose(pG[0:HIST, i * P:(i + 1) * P], hist[:, i, SEQ:SEQ + HIST], keep.ident[:, :])
                for i in range(KC):
                    mm = pe.transpose(pG[0:DB, CC + i * P:CC + (i + 1) * P], hist_s[:, i, :, HIST], keep.ident[:, :])
                mm.then_inc(S["last_psum"], 1)


def stage_sample(nc, a, o, keep):
    LC = LORA + 1
    NG = NPAGE // 4
    JH = NPAGE * NHEAD
    MJ = MT // P
    with Core(nc) as c:
        w_uk = c.sb("ws_uk", [P, KL, NHEAD * NOPE])
        w_uv = c.sb("ws_uv", [P, KL, NHEAD * VH])
        w_ukT = c.sb("ws_ukT", [NOPE, NHEAD, KL, P])
        g_k = c.sb("gs_k", [P, QH])
        table = c.sb("pages", [1, DB * NPAGE], I32)
        spare = keep.mergedT[:, :, :].rearrange("p k n -> p (k n)")
        lat = [spare[:, p * NPAGE * LC:(p + 1) * NPAGE * LC].rearrange("p (n l) -> p n l", l=LC) for p in range(2)]
        krp = [c.sb(f"krp{p}", [P, NPAGE, ROPE]) for p in range(2)]
        mk = [c.sb(f"mk{p}", [P, MJ, MW]) for p in range(2)]
        mvs = [c.sb(f"mvs{p}", [P, MJ, MW]) for p in range(2)]
        q_g = c.sb("q_g", [DB, NHEAD, NOPE])
        q_x = c.sb("q_x", [DB, 4, NHEAD, P])
        q_gT = c.sb("q_gT", [NOPE, NHEAD, DB])
        q_a = c.sb("q_a", [P, KL, DB, NHEAD])
        q_bd = c.sb("q_bd", [P, DB, 4 * NHEAD])
        q_mT = c.sb("q_mT", [P, MH, DB])
        sn = c.sb("sn", [DB, NHEAD])
        prod = c.sb("qk_prod", [DB, NHEAD, QH])
        new = c.sb("new", [1, DB, LC])
        snr = c.sb("snr", [1, DB, NHEAD])
        kg = c.sb("kg", [P, NPAGE, ROPE])
        kc = c.sb("kc", [P, NPAGE, ROPE])
        ks = c.sb("ks", [P, NPAGE, ROPE])
        kr2 = c.sb("kr2", [P, NPAGE, ROPE])
        krot = c.sb("krot", [P, NPAGE, ROPE])
        krT = c.sb("krT", [P, NG, P])
        cT = [c.sb(f"cTs{p}", [P, 4, KL, P]) for p in range(2)]
        sq = [c.sb(f"sqs{p}", [P, NHEAD, NOPE]) for p in range(2)]
        ssk = c.sb("ssk", [P, NPAGE, NHEAD])
        sskr = c.sb("sskr", [P, NPAGE])
        half = c.sb("half", [P, JH])
        rk = c.sb("rk", [P, NPAGE, NHEAD])
        s = c.sb("s_keys", [P, NPAGE, NHEAD])
        pr = c.sb("p_keys", [P, NPAGE, NHEAD])
        m1 = c.sb("m1", [P, 2])
        m2 = c.sb("m2", [1, 2, NHEAD])
        mb = c.sb("mb", [P, 2, NHEAD])
        newb = c.sb("new_b", [1, LC])
        pn = c.sb("p_new", [1, 2, NHEAD])
        mkT = c.sb("mkTs", [P, MJ * MH, P])
        ms = c.sb("ms", [P, MJ, MH])
        mp = c.sb("mps", [P, MJ, MH])
        rsum = c.sb("rsum", [P, MH])
        rden = c.sb("rden", [NHEAD, 1])
        ctx = c.sb("ctx", [NHEAD, LORA])
        ctxT = c.sb("ctxT", [P, KL, NHEAD, DB])
        o_s = c.sb("o_s", [DB, NHEAD * VH])
        onesr = c.sb("onesr", [P, P])
        pT = c.ps("pTs", 1024)
        pK = [c.ps("pKs0"), c.ps("pKs1")]
        pS, pX, pC, pR = c.ps("pSs"), c.ps("pXs"), c.ps("pCs"), c.ps("pRs")
        S = {n: c.sem("s_" + n) for n in """w_in table_in set_v set_a set_p set_d cleared kr_sq rot_v rot_ready krT_psum krT_ready
            cT_psum cT_ready kn_psum sq_ready ss_ready s_psum n_ready r_ready s_ready sT_psum m1_ready m1T_psum m2_ready
            mb_psum mb_ready centred p_ready ctx_psum den ctx_ready ctxT_psum ctxT_ready mkT_psum mkT_ready ms_psum
            ms_ready used mo_psum msum mo_ready end_psum end_v new_in passed""".split()}
        lat_in = [c.sem(f"s_lat_in{p}") for p in range(2)]
        mem_in = [c.sem(f"s_mem_in{p}") for p in range(2)]
        LOADS = 16 * 2 * NPAGE
        with c.block() as block:
            @block.sync
            def _(sp):
                sp.dma_start(table[:, :], a["page_table"].rearrange("(o b) n -> o (b n)", o=1)).then_inc(S["table_in"], 16)
                sp.dma_start(w_uk[:, :, :], a["w_uk"][0].rearrange("(k p) h n -> p k (h n)", p=P)).then_inc(S["w_in"], 16)
                sp.dma_start(w_uv[:, :, :], a["w_uv"][0].rearrange("(k p) h n -> p k (h n)", p=P)).then_inc(S["w_in"], 16)
                sp.dma_start(g_k[:, :], a["g_k_mla"][0].partition_broadcast(P)).then_inc(S["w_in"], 16)
                sp.wait_ge(S["cleared"], 5)
                sp.dma_start(new[0:1, :, 0:LORA], keep.ckv[0:DB, :]).then_inc(S["new_in"], 16)
                sp.wait_ge(S["table_in"], 16)
                with sp.Fori(0, DB // 2) as j:
                    for p in range(2):
                        b = 2 * j + p
                        sp.wait_ge(S["used"], b + 1)
                        for n in range(NPAGE):
                            page = sp.value_load(table[0:1, bass.ds(b * NPAGE + n, 1)], min_val=0, max_val=NPHYS - 1)
                            sp.dma_start(lat[p][:, n, 0:LORA], a["cache_latent"][0][bass.ds(page, 1)].rearrange("o s c -> (o s) c")).then_inc(lat_in[p], 16)
                            sp.dma_start(krp[p][:, n, :], a["cache_krope"][0][bass.ds(page, 1)].rearrange("o s c -> (o s) c")).then_inc(lat_in[p], 16)
                        for dst, name in ((mk, "cache_mem_k"), (mvs, "cache_mem_v")):
                            sp.dma_start(dst[p][:, :, :], a[name][0][bass.ds(b, 1)].rearrange("o (j p) h d -> p (o j) (h d)", p=P)).then_inc(mem_in[p], 16)

            @block.gpsimd
            def _(pool):
                for buf in lat:
                    pool.memset(buf[:, :, LORA:LC], 1.0).then_inc(S["cleared"], 1)
                pool.memset(new[:, :, LORA:LC], 1.0).then_inc(S["cleared"], 1)
                pool.memset(half[:, :], -0.5).then_inc(S["cleared"], 1)
                pool.memset(onesr[:, :], 1.0).then_inc(S["cleared"], 1)
                pool.wait_ge(S["set_v"], 4)
                pool.dma_start(snr[0:1, :, :], sn[:, :]).then_inc(S["set_p"], 16)
                pool.sem_inc(S["used"], 2)
                with pool.Fori(0, DB) as b:
                    pool.wait_ge(S["n_ready"], 1 + b + 1)
                    pool.tensor_tensor(rk[:, :, :], ssk[:, :, :], half[:, :].rearrange("p (j h) -> p j h", h=NHEAD), ALU.pow).then_inc(S["r_ready"], 1)
                pool.wait_ge(S["set_p"], 16)

            @block.scalar
            def _(act):
                c.start_at_one(act, S, "n_ready s_psum ss_ready krT_psum r_ready mkT_ready m1_ready s_ready ctxT_ready mo_ready")
                act.wait_ge(S["set_d"], 1)
                act.activation(w_ukT[:, 0:4, :, :], pT[0:NOPE, :].rearrange("p (h k n) -> p h k n", h=4, k=KL), ACT.Copy).then_inc(S["set_a"], 1)
                act.wait_ge(S["set_d"], 2)
                act.activation(w_ukT[:, 4:8, :, :], pT[0:NOPE, :].rearrange("p (h k n) -> p h k n", h=4, k=KL), ACT.Copy).then_inc(S["set_a"], 1)
                act.wait_ge(S["set_d"], 3)
                act.activation(q_gT[:, :, :], pR[0:NOPE, 0:NHEAD * DB].rearrange("p (h b) -> p h b", h=NHEAD), ACT.Copy)
                act.activation(q_bd[:, :, :].rearrange("p b e -> p e b"), pS[:, 0:4 * NHEAD * DB].rearrange("p (e b) -> p e b", b=DB), ACT.Copy)
                act.activation(q_mT[:, :, :], pC[:, 0:MH * DB].rearrange("p (h b) -> p h b", h=MH), ACT.Copy).then_inc(S["set_a"], 1)
                act.wait_ge(S["set_d"], 4)
                act.activation(q_a[:, :, :, :].rearrange("p k b h -> p k h b"), pX[:, 0:KL * NHEAD * DB].rearrange("p (k h b) -> p k h b", k=KL, h=NHEAD),
                               ACT.Copy).then_inc(S["set_a"], 1)
                act.wait_ge(S["set_p"], 16)

                def sequence(j, p):
                    b = 2 * j + p
                    act.wait_ge(lat_in[p], LOADS * j + LOADS)
                    act.wait_ge(S["n_ready"], 1 + b)
                    act.activation(kr2[:, :, :], krp[p][:, :, :], ACT.Square).then_inc(S["kr_sq"], 1)

                    def take(g):
                        act.wait_ge(S["cT_psum"], NG * b + g + 1)
                        if g >= 2:
                            act.wait_ge(S["kn_psum"], NPAGE * b + 4 * (g - 1))
                        else:
                            act.wait_ge(S["s_psum"], 1 + b)
                        act.activation(cT[g % 2][:, :, :, :], pT[:, :].rearrange("p (n k q) -> p n k q", n=4, k=KL), ACT.Copy).then_inc(S["cT_ready"], 1)

                    take(0)
                    act.wait_ge(S["krT_psum"], 1 + b + 1)
                    act.activation(krT[:, :, :], pR[:, :].rearrange("p (g q) -> p g q", g=NG), ACT.Copy).then_inc(S["krT_ready"], 1)
                    for n in range(NPAGE):
                        if n % 4 == 1 and n // 4 + 1 < NG:
                            take(n // 4 + 1)
                        act.wait_ge(S["kn_psum"], NPAGE * b + n + 1)
                        if n >= 2:
                            act.wait_ge(S["ss_ready"], 1 + NPAGE * b + n - 1)
                        else:
                            act.wait_ge(S["ss_ready"], 1 + NPAGE * b)
                        act.activation(sq[n % 2][:, :, :], heads(pK[n % 2][:, :], NHEAD), ACT.Square).then_inc(S["sq_ready"], 1)
                    act.wait_ge(S["mkT_psum"], b + 1)
                    act.activation(mkT[:, :, :], pT[:, :].rearrange("p (n q) -> p n q", q=P), ACT.Copy).then_inc(S["mkT_ready"], 1)
                    act.wait_ge(S["centred"], b + 1)
                    act.wait_ge(S["new_in"], 16)
                    act.activation(newb[:, :], new[0:1, b, :], ACT.Copy)
                    act.activation(pr[:, :, :], s[:, :, :], ACT.Exp, scale=SC_MLA)
                    act.activation(mp[:, :, :], ms[:, :, :], ACT.Exp, scale=SC_MEM)
                    act.activation(pn[0:1, 1, :], pn[0:1, 0, :], ACT.Exp, scale=SC_MLA).then_inc(S["p_ready"], 1)

                with act.Fori(0, DB // 2) as j:
                    for p in range(2):
                        sequence(j, p)

            @block.vector
            def _(v):
                v.wait_ge(S["w_in"], 48)
                v.wait_ge(S["cleared"], 5)
                q3, k3 = heads(keep.qn[0:DB, :], NHEAD), heads(keep.kn[0:DB, :], NHEAD)
                v.memset(m2[:, :, :], 0.0)
                v.memset(q_x[:, :, :, :], 0.0).then_inc(S["set_v"], 1)
                v.tensor_tensor(prod[:, :, :], q3, k3, ALU.mult)
                v.tensor_tensor(q_g[:, :, :], q3[:, :, 0:NOPE], spread(g_k[0:DB, 0:NOPE], NHEAD), ALU.mult).then_inc(S["set_v"], 1)
                v.wait_ge(S["set_v"], 2)
                for i in range(4):
                    e = v.tensor_copy(q_x[:, i, :, i * ROPE:(i + 1) * ROPE], q3[:, :, NOPE:QH])
                e.then_inc(S["set_v"], 1)
                v.tensor_reduce(sn[:, :], prod[:, :, :], AX.X, ALU.add).then_inc(S["set_v"], 1)
                v.wait_ge(S["set_p"], 16)

                def sequence(j, p):
                    b = 2 * j + p
                    own = Steps(S["rot_v"], b, 3)
                    cos, sin = keep.cos[:, 0:NPAGE, :], keep.sin[:, 0:NPAGE, :]
                    v.wait_ge(lat_in[p], LOADS * j + LOADS)
                    own.mark(v.tensor_tensor(kg[:, :, :], krp[p][:, :, :], spread(g_k[:, NOPE:QH], NPAGE), ALU.mult))
                    own.wait(v)
                    v.tensor_tensor(kc[:, :, :], kg[:, :, :], cos, ALU.mult)
                    own.mark(v.tensor_tensor(ks[:, :, :], kg[:, :, :], sin, ALU.mult))
                    own.wait(v)
                    v.wait_ge(S["krT_psum"], 1 + b)
                    v.tensor_tensor(krot[:, :, 0:16], kc[:, :, 0:16], ks[:, :, 16:32], ALU.subtract)
                    v.tensor_tensor(krot[:, :, 16:32], kc[:, :, 16:32], ks[:, :, 0:16], ALU.add).then_inc(S["rot_ready"], 1)
                    v.wait_ge(S["kr_sq"], b + 1)
                    own.mark(v.tensor_reduce(sskr[:, :], kr2[:, :, :], AX.X, ALU.add))
                    v.wait_ge(S["r_ready"], 1 + b)
                    for n in range(NPAGE):
                        v.wait_ge(S["sq_ready"], NPAGE * b + n + 1)
                        v.tensor_reduce(ssk[:, n, :], sq[n % 2][:, :, :], AX.X, ALU.add).then_inc(S["ss_ready"], 1)
                    v.wait_ge(S["ss_ready"], 1 + NPAGE * b + NPAGE)
                    own.wait(v)
                    own.end()
                    v.tensor_tensor(ssk[:, :, :], ssk[:, :, :], spread(sskr[:, :], NHEAD, 2), ALU.add).then_inc(S["s_ready"], 1)
                    v.wait_ge(S["s_ready"], 1 + 3 * b + 1)
                    v.tensor_scalar(ssk[:, :, :], ssk[:, :, :], 1.0 / QH, EPS, ALU.mult, ALU.add).then_inc(S["n_ready"], 1)
                    v.wait_ge(S["ms_psum"], b + 1)
                    v.tensor_copy(ms[:, :, :], pX[:, 0:MJ * MH].rearrange("p (j h) -> p j h", j=MJ)).then_inc(S["s_ready"], 1)
                    v.wait_ge(S["r_ready"], 1 + b + 1)
                    v.wait_ge(S["s_psum"], 1 + b + 1)
                    v.tensor_tensor(s[:, :, :], pS[:, 0:JH].rearrange("p (j h) -> p j h", h=NHEAD), rk[:, :, :], ALU.mult).then_inc(S["s_ready"], 1)
                    v.wait_ge(S["sT_psum"], b + 1)
                    v.tensor_reduce(m1[:, 0:1], pR[:, 0:P], AX.X, ALU.max)
                    v.tensor_reduce(m1[0:MJ * MH, 1:2], pR[0:MJ * MH, P:2 * P], AX.X, ALU.max).then_inc(S["m1_ready"], 1)
                    v.wait_ge(S["m1T_psum"], b + 1)
                    v.tensor_reduce(m2[0:1, 1, :], pX[0:1, 64:64 + JH].rearrange("p (j h) -> p h j", h=NHEAD), AX.X, ALU.max)
                    v.tensor_reduce(m2[0:1, 0, 0:MH], pX[0:1, 192:192 + MJ * MH].rearrange("p (j h) -> p h j", h=MH), AX.X, ALU.max).then_inc(S["ms_ready"], 1)
                    v.wait_ge(S["ms_ready"], 2 * b + 1)
                    v.tensor_tensor(m2[0:1, 1, :], m2[0:1, 1, :], snr[0:1, b, :], ALU.max).then_inc(S["m2_ready"], 1)
                    v.wait_ge(S["mb_psum"], b + 1)
                    v.tensor_copy(mb[:, :, :], pX[:, 256:272].rearrange("p (w h) -> p w h", w=2)).then_inc(S["ms_ready"], 1)
                    v.wait_ge(S["ms_ready"], 2 * b + 2)
                    v.tensor_tensor(s[:, :, :], s[:, :, :], spread(mb[:, 1, :], NPAGE), ALU.subtract)
                    v.tensor_tensor(ms[:, :, :], ms[:, :, :], spread(mb[:, 0, 0:MH], MJ), ALU.subtract)
                    v.tensor_tensor(pn[0:1, 0, :], snr[0:1, b, :], mb[0:1, 1, :], ALU.subtract).then_inc(S["centred"], 1)
                    v.wait_ge(S["ctx_psum"], b + 1)
                    v.reciprocal(rden[:, :], pC[0:NHEAD, LORA:LC]).then_inc(S["used"], 1)
                    v.reciprocal(rsum[:, :], pC[:, 320:320 + MH]).then_inc(S["den"], 1)
                    v.wait_ge(S["den"], b + 1)
                    v.tensor_scalar(ctx[:, :], pC[0:NHEAD, 0:LORA], rden[:, 0:1], None, ALU.mult).then_inc(S["ctx_ready"], 1)
                    v.tensor_tensor(keep.moT_s[:, :, b], pC[:, 328:328 + MH], rsum[:, :], ALU.mult).then_inc(S["mo_ready"], 1)
                    v.wait_ge(S["ctxT_psum"], b + 1)
                    v.tensor_copy(ctxT[:, :, :, b], pX[:, 288:304].rearrange("p (k h) -> p k h", k=KL)).then_inc(S["ctxT_ready"], 1)

                with v.Fori(0, DB // 2) as j:
                    for p in range(2):
                        sequence(j, p)
                v.wait_ge(S["end_psum"], 1)
                v.tensor_copy(o_s[:, :], pK[0][0:DB, :]).then_inc(S["end_v"], 1)
                v.wait_ge(S["end_psum"], 2)
                v.tensor_copy(keep.oT_s[:, :, :], pX[:, 0:4 * DB].rearrange("p (k b) -> p k b", k=4)).then_inc(S["end_v"], 1)

            @block.tensor
            def _(pe):
                I = keep.ident
                pe.wait_ge(S["w_in"], 48)
                for half_ in range(2):
                    pe.wait_ge(S["set_a"], half_)
                    for h in range(4):
                        for k in range(KL):
                            at = (h * KL + k) * P
                            hh = 4 * half_ + h
                            mm = pe.transpose(pT[0:NOPE, at:at + P], w_uk[:, k, hh * NOPE:(hh + 1) * NOPE], I[:, :])
                    mm.then_inc(S["set_d"], 1)
                pe.wait_ge(S["set_v"], 4)
                I8 = I[0:DB, 0:DB]
                for h in range(NHEAD):
                    pe.transpose(pR[0:NOPE, h * DB:(h + 1) * DB], q_g[:, h, :], I8)
                for i in range(4):
                    for h in range(NHEAD):
                        at = (i * NHEAD + h) * DB
                        pe.transpose(pS[:, at:at + DB], q_x[:, i, h, :], I8)
                for h in range(MH):
                    mm = pe.transpose(pC[:, h * DB:(h + 1) * DB], keep.qmn[0:DB, h * P:(h + 1) * P], I8)
                mm.then_inc(S["set_d"], 1)
                pe.wait_ge(S["set_a"], 3)
                for k in range(KL):
                    for h in range(NHEAD):
                        at = (k * NHEAD + h) * DB
                        mm = pe.matmul(pX[:, at:at + DB], w_ukT[:, h, k, :], q_gT[:, h, :], start=True, stop=True)
                mm.then_inc(S["set_d"], 1)
                pe.wait_ge(S["set_a"], 4)

                def sequence(j, p):
                    b = 2 * j + p
                    pe.wait_ge(lat_in[p], LOADS * j + LOADS)

                    def turn(g):
                        for i in range(4):
                            for k in range(KL):
                                mm = pe.transpose(pT[:, (i * KL + k) * P:(i * KL + k + 1) * P], lat[p][:, 4 * g + i, k * P:(k + 1) * P], I[:, :])
                        mm.then_inc(S["cT_psum"], 1)

                    pe.wait_ge(S["mkT_ready"], 1 + b)
                    turn(0)
                    pe.wait_ge(S["rot_ready"], b + 1)
                    pe.wait_ge(S["m1_ready"], 1 + b)
                    for g in range(NG):
                        mm = pe.transpose(pR[:, g * P:(g + 1) * P], krot[:, 4 * g:4 * g + 4, :].rearrange("p n r -> p (n r)"), I[:, :])
                    mm.then_inc(S["krT_psum"], 1)
                    pe.wait_ge(S["krT_ready"], b + 1)
                    pe.wait_ge(S["s_ready"], 1 + 3 * b)
                    for g in range(NG):
                        pe.wait_ge(S["cT_ready"], NG * b + g + 1)
                        if g + 1 < NG:
                            turn(g + 1)
                        pe.matmul(pS[:, g * 32:(g + 1) * 32], krT[:, g, :], q_bd[:, b, :], start=True, stop=False, skip_group_check=True)
                        for i in range(4):
                            n = 4 * g + i
                            if n >= 2:
                                pe.wait_ge(S["sq_ready"], NPAGE * b + n - 1)
                            for k in range(KL):
                                mm = pe.matmul(pK[n % 2][:, :], cT[g % 2][:, i, k, :], w_uk[:, k, :], start=k == 0, stop=k == KL - 1)
                            mm.then_inc(S["kn_psum"], 1)
                            for k in range(KL):
                                mm = pe.matmul(pS[:, n * NHEAD:(n + 1) * NHEAD], cT[g % 2][:, i, k, :], q_a[:, k, b, :], start=False, stop=k == KL - 1,
                                               skip_group_check=True)
                    mm.then_inc(S["s_psum"], 1)
                    pe.wait_ge(mem_in[p], 32 * j + 32)
                    for n in range(MJ * MH):
                        mm = pe.transpose(pT[:, n * P:(n + 1) * P], mk[p][:, n // MH, (n % MH) * P:(n % MH + 1) * P], I[:, :])
                    mm.then_inc(S["mkT_psum"], 1)
                    pe.wait_ge(S["mkT_ready"], 1 + b + 1)
                    pe.wait_ge(S["ctxT_ready"], 1 + b)
                    for n in range(MJ * MH):
                        mm = pe.matmul(pX[:, n:n + 1], mkT[:, n, :], q_mT[:, n % MH, b:b + 1] if isinstance(b, int) else q_mT[:, n % MH, bass.ds(b, 1)],
                                       start=True, stop=True)
                    mm.then_inc(S["ms_psum"], 1)
                    pe.wait_ge(S["s_ready"], 1 + 3 * b + 3)
                    pe.transpose(pR[:, 0:P], s[:, :, :].rearrange("p j h -> p (j h)"), I[:, :])
                    pe.transpose(pR[0:MJ * MH, P:2 * P], ms[:, :, :].rearrange("p j h -> p (j h)"), I[:, :]).then_inc(S["sT_psum"], 1)
                    pe.wait_ge(S["m1_ready"], 1 + b + 1)
                    pe.transpose(pX[0:1, 64:64 + JH], m1[:, 0:1], I[:, :])
                    pe.transpose(pX[0:1, 192:192 + MJ * MH], m1[0:MJ * MH, 1:2], I[0:MJ * MH, 0:MJ * MH]).then_inc(S["m1T_psum"], 1)
                    pe.wait_ge(S["m2_ready"], b + 1)
                    pe.matmul(pX[:, 256:272], onesr[0:1, :], m2[0:1, :, :].rearrange("p w h -> p (w h)"), start=True, stop=True).then_inc(S["mb_psum"], 1)
                    pe.wait_ge(S["p_ready"], b + 1)
                    pe.wait_ge(S["mo_ready"], 1 + b)
                    for n in range(NPAGE):
                        pe.matmul(pC[0:NHEAD, 0:LC], pr[:, n, :], lat[p][:, n, :], start=n == 0, stop=False)
                    pe.matmul(pC[0:NHEAD, 0:LC], pn[0:1, 1, :], newb[:, :], start=False, stop=True)
                    for n in range(MJ):
                        pe.matmul(pC[:, 320:320 + MH], onesr[:, :], mp[:, n, :], start=n == 0, stop=n == MJ - 1)
                    for h in range(MH):
                        for n in range(MJ):
                            mm = pe.matmul(pC[:, 328 + h:329 + h], mvs[p][:, n, h * P:(h + 1) * P], mp[:, n, h:h + 1], start=n == 0, stop=n == MJ - 1)
                    mm.then_inc(S["ctx_psum"], 1)
                    pe.wait_ge(S["ctx_ready"], b + 1)
                    pe.sem_inc(S["passed"], 1)
                    for k in range(KL):
                        mm = pe.transpose(pX[:, 288 + k * NHEAD:288 + (k + 1) * NHEAD], ctx[:, k * P:(k + 1) * P], I8)
                    mm.then_inc(S["ctxT_psum"], 1)

                with pe.Fori(0, DB // 2) as j:
                    for p in range(2):
                        sequence(j, p)
                pe.wait_ge(S["ctxT_ready"], 1 + DB)
                for h in range(NHEAD):
                    for k in range(KL):
                        mm = pe.matmul(pK[0][0:DB, h * VH:(h + 1) * VH], ctxT[:, k, h, :], w_uv[:, k, h * VH:(h + 1) * VH], start=k == 0, stop=k == KL - 1)
                mm.then_inc(S["end_psum"], 1)
                pe.wait_ge(S["end_v"], 1)
                for k in range(4):
                    mm = pe.transpose(pX[:, k * DB:(k + 1) * DB], o_s[:, k * P:(k + 1) * P], I8)
                mm.then_inc(S["end_psum"], 1)


def stage_merge(nc, a, keep):
    GROUPS = ((0, 512), (512, 512), (SEQ, DB))
    NU = 3 * len(GROUPS)
    with Core(nc) as c:
        wg = [c.sb(f"w_gate{p}", [P, 3, KD, P]) for p in range(2)]
        wo = [c.sb(f"w_o{p}", [P, 3, 4, P]) for p in range(2)]
        oT = c.sb("oT", [P, 2, 4, TOK])
        sig = c.sb("gate_sig", [P, 3, 512])
        tmp = c.sb("gated", [P, 512])
        pG = [c.ps(f"pGate{i}") for i in range(3)]
        pY = [c.ps(f"pBranch{i}") for i in range(3)]
        S = {n: c.sem("m_" + n) for n in "o_in o_sample unit_psum sig_ready unit_used gated".split()}
        w_in = [c.sem(f"m_w_in{p}") for p in range(2)]
        w_used = c.sem("m_w_used")
        with c.block() as block:
            @block.sync
            def _(sp):
                def weights(j, p):
                    cc = 2 * j + p
                    sp.wait_ge(w_used, cc + 1)
                    for g in range(3):
                        sp.dma_start(wg[p][:, g, :, :], a["w_in"][0][:, C_GATE + g * D:C_GATE + (g + 1) * D].rearrange("(k p) n -> p k n", p=P)[:, :, bass.ds(cc * P, P)]).then_inc(w_in[p], 16)
                    for g, name in enumerate(("w_o_mla", "w_conv_out", "w_o_mem")):
                        sp.dma_start(wo[p][:, g, :, :], a[name][0].rearrange("(k p) n -> p k n", p=P)[:, :, bass.ds(cc * P, P)]).then_inc(w_in[p], 16)

                with sp.Fori(0, KD // 2) as j:
                    for p in range(2):
                        weights(j, p)

            @block.gpsimd
            def _(pool):
                pool.sem_inc(w_used, 2)
                for w in range(2):
                    for k in range(4):
                        pool.dma_start(oT[:, w, k, 0:SEQ].rearrange("p (t n) -> p t n", t=NT),
                                       keep.o_dram[:, :, w, k * P:(k + 1) * P].rearrange("t p n -> p t n")).then_inc(S["o_in"], 16)
                pool.tensor_copy(oT[:, 0, :, SEQ:TOK], keep.oT_s[:, :, :]).then_inc(S["o_sample"], 1)
                pool.tensor_copy(oT[:, 1, :, SEQ:TOK], keep.moT_s[:, :, :]).then_inc(S["o_sample"], 1)

            @block.scalar
            def _(act):
                c.start_at_one(act, S, "gated")
                with act.Fori(0, KD // 2) as j:
                    for p in range(2):
                        for u in range(NU):
                            n = GROUPS[u // 3][1]
                            act.wait_ge(S["unit_psum"], NU * (2 * j + p) + u + 1)
                            act.activation(sig[:, u % 3, 0:n], pG[u % 3][:, 0:n], ACT.Sigmoid).then_inc(S["sig_ready"], 1)

            @block.vector
            def _(v):
                v.sem_inc(S["unit_used"], 3)
                with v.Fori(0, KD // 2) as j:
                    for p in range(2):
                        cc = 2 * j + p
                        for u in range(NU):
                            at, n = GROUPS[u // 3]
                            merged = keep.mergedT[:, cc, at:at + n]
                            done = 2 * 3 * cc + 2 * (u // 3)
                            v.wait_ge(S["sig_ready"], NU * cc + u + 1)
                            if u % 3 == 0:
                                v.tensor_tensor(merged, sig[:, 0, 0:n], pY[0][:, 0:n], ALU.mult).then_inc(S["unit_used"], 1)
                                continue
                            v.wait_ge(S["gated"], 1 + done + u % 3 - 1)
                            v.tensor_tensor(tmp[:, 0:n], sig[:, u % 3, 0:n], pY[u % 3][:, 0:n], ALU.mult).then_inc(S["unit_used"], 1)
                            v.wait_ge(S["unit_used"], 3 + NU * cc + u + 1)
                            v.tensor_tensor(merged, merged, tmp[:, 0:n], ALU.add).then_inc(S["gated"], 1)

            @block.tensor
            def _(pe):
                pe.wait_ge(S["o_in"], 128)
                pe.wait_ge(S["o_sample"], 2)
                branch = (lambda at, n, k: oT[:, 0, k, at:at + n], lambda at, n, k: keep.convT[:, k, at:at + n], lambda at, n, k: oT[:, 1, k, at:at + n])
                with pe.Fori(0, KD // 2) as j:
                    for p in range(2):
                        pe.wait_ge(w_in[p], 96 * j + 96)
                        for u in range(NU):
                            at, n = GROUPS[u // 3]
                            g = u % 3
                            pe.wait_ge(S["unit_used"], NU * (2 * j + p) + u + 1)
                            for k in range(4):
                                pe.matmul(pY[g][:, 0:n], wo[p][:, g, k, :], branch[g](at, n, k), start=k == 0, stop=k == 3)
                            for k in range(KD):
                                mm = pe.matmul(pG[g][:, 0:n], wg[p][:, g, k, :], keep.hT[:, k, at:at + n], start=k == 0, stop=k == KD - 1)
                            mm.then_inc(S["unit_psum"], 1)
                        pe.wait_ge(S["unit_psum"], NU * (2 * j + p) + NU)
                        pe.sem_inc(w_used, 1)


CAP = 192
TRASH = CAP
ROWS = TOK + TRASH
BIG = 1.0e6


def stage_mixer(nc, a, keep):
    NTT = NT + 1
    with Core(nc) as c:
        w_out = c.sb("w_out", [P, KD, D])
        w_r = c.sb("w_router", [P, KD, NE])
        w_sgu = c.sb("w_sgu", [P, KD, 2 * DE])
        w_sd = c.sb("w_sd", [P, 2, D])
        g_f = c.sb("g_ffn", [P, D])
        b_r = c.sb("b_router", [P, NE])
        before = c.sb("before", [P, P])
        ones = c.sb("ones_f", [P, P])
        valid = c.sb("valid", [P, 2])
        zero = c.sb("zero", [P, D])
        x = c.sb("x_f", [P, D])
        x2 = c.sb("x2", [P, D])
        h2 = c.sb("h2", [P, D])
        acc = c.sb("acc", [P, D])
        mT = c.sb("mT", [P, KD, P])
        hT = c.sb("h2T", [P, KD, P])
        junk = c.sb("junk_f", [P, D])
        ss = c.sb("ss_f", [P, 1])
        n1 = c.sb("n_f", [P, 1])
        r1 = c.sb("r_f", [P, 1])
        sc = c.sb("scores", [P, NE])
        bi = c.sb("biased", [P, NE])
        rep = c.sb("replaced", [P, NE])
        m8 = c.sb("top8", [P, 8])
        mask = c.sb("chosen", [P, NE])
        wsum = c.sb("wsum", [P, 1])
        wr = c.sb("wrecip", [P, 1])
        wt = c.sb("weights", [P, NE])
        cum = c.sb("cum", [P, NE])
        rk = c.sb("rank_raw", [P, NE])
        sg = c.sb("sh_sig", [P, DE])
        sgg = c.sb("sh_gate", [P, DE])
        sh = c.sb("sh_h", [P, DE])
        shT = c.sb("sh_hT", [P, 2, P])
        cst = c.sb("val_consts", [P, NTT, 3])
        thr = c.sb("thresholds", [1, 6])
        over = c.sb("over", [1, 6])
        cmax = c.sb("cmax", [1, 2])
        pX, pT, pD = c.ps("pXf", 1024), c.ps("pTf", 1024), c.ps("pDf", 1024)
        pR, pGU = c.ps("pRf"), c.ps("pGUf")
        S = {n: c.sem("f_" + n) for n in """w_in small_in set_p trash_in x_in x_cleared mT_ready x2_psum x2_ready squares
            mean rsq h2_ready h2_stored hT_psum hT_ready route_psum sc_ready steps mask_ready rank_psum tab_ready
            sig_ready sh_ready shT_psum shT_ready down_psum acc_ready acc_stored count passed""".split()}
        VS = 13
        with c.block() as block:
            @block.sync
            def _(sp):
                for dst, src in ((g_f[:, :], a["g_ffn_norm"][0].partition_broadcast(P)), (b_r[:, :], a["b_router"][0].partition_broadcast(P)),
                                 (before[:, :], a["k_before"]), (valid[:, :], a["k_valid"]), (cst[:, :, :], a["k_vals"]), (thr[:, :], a["k_thresholds"])):
                    sp.dma_start(dst, src).then_inc(S["small_in"], 16)
                sp.dma_start(w_out[:, :, :], a["w_out"][0].rearrange("(k p) n -> p k n", p=P)).then_inc(S["w_in"], 16)
                sp.dma_start(w_r[:, :, :], a["w_router"][0].rearrange("(k p) n -> p k n", p=P)).then_inc(S["w_in"], 16)
                sp.dma_start(w_sgu[:, :, 0:DE], a["w_s_gate"][0].rearrange("(k p) n -> p k n", p=P)).then_inc(S["w_in"], 16)
                sp.dma_start(w_sgu[:, :, DE:2 * DE], a["w_s_up"][0].rearrange("(k p) n -> p k n", p=P)).then_inc(S["w_in"], 16)
                sp.dma_start(w_sd[:, :, :], a["w_s_down"][0].rearrange("(k p) n -> p k n", p=P)).then_inc(S["w_in"], 16)
                sp.wait_ge(S["set_p"], 2)
                for dram in (keep.h_dram, keep.acc_dram):
                    for at in range(TOK, ROWS, 64):
                        sp.dma_start(dram[at:at + 64, :], zero[0:64, :]).then_inc(S["trash_in"], 16)

                def tile(t, src, rows, dst):
                    sp.wait_ge(S["x2_ready"], 1 + t)
                    sp.dma_start(x[0:rows, :], src).then_inc(S["x_in"], 16)
                    sp.wait_ge(S["h2_ready"], t + 1)
                    sp.dma_start(keep.h_dram[dst, :], h2[0:rows, :]).then_inc(S["h2_stored"], 16)
                    sp.wait_ge(S["acc_ready"], 1 + t + 1)
                    sp.dma_start(keep.acc_dram[dst, :], acc[0:rows, :]).then_inc(S["acc_stored"], 16)

                with sp.Fori(0, NT) as t:
                    tile(t, a["x_prompt"][0][bass.ds(t * P, P), :], P, bass.ds(t * P, P))
                sp.wait_ge(S["x_cleared"], 1)
                tile(NT, a["x_sample"].rearrange("b s d -> (b s) d"), DB, slice(SEQ, TOK))
                sp.wait_ge(S["h2_stored"], 1 + 16 * NTT)
                sp.wait_ge(S["acc_stored"], 1 + 16 * NTT)
                sp.wait_ge(S["trash_in"], 16 * 2 * (TRASH // 64))

            @block.gpsimd
            def _(pool):
                pool.memset(ones[:, :], 1.0).then_inc(S["set_p"], 1)
                pool.memset(zero[:, :], 0.0).then_inc(S["set_p"], 1)
                pool.memset(cum[:, :], 0.0).then_inc(S["set_p"], 1)
                with pool.Fori(0, NTT) as t:
                    pool.wait_ge(S["mean"], t + 1)
                    pool.tensor_tensor(r1[:, :], n1[:, :], keep.mhalf[:, 0:1], ALU.pow).then_inc(S["rsq"], 1)

            @block.scalar
            def _(act):
                c.start_at_one(act, S, "x2_ready x2_psum tab_ready h2_stored acc_stored shT_ready count sh_ready acc_ready")
                def tile(t, cols, width):
                    act.wait_ge(S["x2_psum"], 1 + t)
                    if width < P:
                        act.wait_ge(S["x_cleared"], 1)
                    act.activation(mT[:, :, 0:width], keep.mergedT[:, :, cols], ACT.Copy).then_inc(S["mT_ready"], 1)
                    act.wait_ge(S["x2_ready"], 1 + t + 1)
                    act.activation(junk[:, :], x2[:, :], ACT.Square, accum_out=ss[:, :]).then_inc(S["squares"], 1)
                    act.wait_ge(S["hT_psum"], t + 1)
                    act.activation(hT[:, :, :], pT[:, :].rearrange("p (k n) -> p k n", k=KD), ACT.Copy).then_inc(S["hT_ready"], 1)
                    act.wait_ge(S["route_psum"], 2 * t + 1)
                    act.wait_ge(S["tab_ready"], 1 + t)
                    act.activation(sc[:, :], pR[:, 0:NE], ACT.Sigmoid).then_inc(S["sc_ready"], 1)
                    act.wait_ge(S["route_psum"], 2 * t + 2)
                    act.activation(sg[:, :], pGU[:, 0:DE], ACT.Sigmoid).then_inc(S["sig_ready"], 1)
                    act.wait_ge(S["shT_psum"], t + 1)
                    act.activation(shT[:, :, :], pT[:, 0:2 * P].rearrange("p (k n) -> p k n", k=2), ACT.Copy).then_inc(S["shT_ready"], 1)

                with act.Fori(0, NT) as t:
                    tile(t, bass.ds(t * P, P), P)
                tile(NT, slice(SEQ, TOK), DB)

            @block.vector
            def _(v):
                v.wait_ge(S["small_in"], 96)
                v.wait_ge(S["set_p"], 3)
                v.tensor_copy(keep.vals[:, :, 0:3, :], spread(cst[:, :, :], NE, 3))

                def tile(t, sample):
                    own = Steps(S["steps"], t, VS)
                    v.wait_ge(S["x_in"], 16 * t + 16)
                    v.wait_ge(S["x2_psum"], 1 + t + 1)
                    v.tensor_tensor(x2[:, :], pX[:, :], x[:, :], ALU.add).then_inc(S["x2_ready"], 1)
                    v.wait_ge(S["squares"], t + 1)
                    v.tensor_scalar(n1[:, :], ss[:, :], 1.0 / D, EPS, ALU.mult, ALU.add).then_inc(S["mean"], 1)
                    v.wait_ge(S["rsq"], t + 1)
                    v.wait_ge(S["h2_stored"], 1 + 16 * t)
                    v.scalar_tensor_tensor(h2[:, :], x2[:, :], r1[:, 0:1], g_f[:, :], ALU.mult, ALU.mult).then_inc(S["h2_ready"], 1)
                    v.wait_ge(S["sc_ready"], t + 1)
                    own.mark(v.tensor_tensor(bi[:, :], sc[:, :], b_r[:, :], ALU.add))
                    own.wait(v)
                    v.sem_inc(S["passed"], 1)
                    own.mark(v.max(out=m8[:, :], in_=bi[:, :]))
                    own.wait(v)
                    v.sem_inc(S["passed"], 1)
                    own.mark(v.match_replace(out=rep[:, :], in_to_replace=m8[:, :], in_values=bi[:, :], imm_value=-3.0e38))
                    own.wait(v)
                    own.mark(v.tensor_tensor(mask[:, :], rep[:, :], bi[:, :], ALU.not_equal))
                    own.wait(v)
                    v.tensor_scalar(mask[:, :], mask[:, :], valid[:, sample:sample + 1], None, ALU.mult).then_inc(S["mask_ready"], 1)
                    v.wait_ge(S["mask_ready"], t + 1)
                    own.mark(v.tensor_tensor(wt[:, :], sc[:, :], mask[:, :], ALU.mult))
                    own.wait(v)
                    own.mark(v.tensor_reduce(wsum[:, :], wt[:, :], AX.X, ALU.add))
                    own.wait(v)
                    own.mark(v.tensor_scalar(wsum[:, :], wsum[:, :], 1e-30 if sample else 0.0, None, ALU.add))
                    own.wait(v)
                    own.mark(v.reciprocal(wr[:, :], wsum[:, :]))
                    own.wait(v)
                    own.mark(v.tensor_scalar(wt[:, :], wt[:, :], wr[:, 0:1], 2.5, ALU.mult, ALU.mult))
                    own.wait(v)
                    for i in range(3, 6):
                        part = keep.vals[:, t, i, :]
                        if i < 5:
                            own.mark(v.tensor_copy(part, wt[:, :]))
                            own.wait(v)
                            own.mark(v.tensor_tensor(wt[:, :], wt[:, :], part, ALU.subtract))
                            own.wait(v)
                        else:
                            v.tensor_copy(part, wt[:, :]).then_inc(S["tab_ready"], 1)
                    v.wait_ge(S["rank_psum"], t + 1)
                    v.tensor_tensor(rk[:, :], pR[:, 128:128 + NE], cum[:, :], ALU.add).then_inc(S["count"], 1)
                    v.wait_ge(S["count"], 1 + 3 * t + 1)
                    v.tensor_tensor(cum[:, :], pR[:, 256:256 + NE], cum[:, :], ALU.add)
                    v.scalar_tensor_tensor(rk[:, :], rk[:, :], BIG, mask[:, :], ALU.add, ALU.mult).then_inc(S["count"], 1)
                    v.wait_ge(S["count"], 1 + 3 * t + 2)
                    v.tensor_scalar(keep.rank[:, t, :], rk[:, :], -BIG, None, ALU.add).then_inc(S["count"], 1)
                    v.wait_ge(S["sig_ready"], t + 1)
                    v.tensor_tensor(sgg[:, :], sg[:, :], pGU[:, 0:DE], ALU.mult).then_inc(S["sh_ready"], 1)
                    v.wait_ge(S["sh_ready"], 1 + 2 * t + 1)
                    v.tensor_tensor(sh[:, :], sgg[:, :], pGU[:, DE:2 * DE], ALU.mult).then_inc(S["sh_ready"], 1)
                    v.wait_ge(S["down_psum"], t + 1)
                    v.wait_ge(S["acc_stored"], 1 + 16 * t)
                    v.tensor_tensor(acc[:, :], pD[:, :], x2[:, :], ALU.add).then_inc(S["acc_ready"], 1)
                    own.end()

                with v.Fori(0, NT) as t:
                    tile(t, 0)
                v.wait_ge(S["x2_psum"], 1 + NT)
                v.memset(mT[:, :, :], 0.0)
                v.memset(x[:, :], 0.0).then_inc(S["x_cleared"], 1)
                tile(NT, 1)
                v.wait_ge(S["count"], 1 + 3 * NTT)
                v.tensor_reduce(cmax[:, 0:1], cum[0:1, :], AX.X, ALU.max).then_inc(S["count"], 1)
                v.wait_ge(S["count"], 1 + 3 * NTT + 1)
                v.tensor_scalar(over[:, :], thr[:, :], cmax[:, 0:1], None, ALU.is_lt).then_inc(S["count"], 1)
                v.wait_ge(S["count"], 1 + 3 * NTT + 2)
                v.tensor_reduce(cmax[:, 1:2], over[:, :], AX.X, ALU.add).then_inc(S["count"], 1)
                v.wait_ge(S["count"], 1 + 3 * NTT + 3)
                v.tensor_copy(keep.passes[:, :], cmax[:, 1:2]).then_inc(S["count"], 1)

            @block.tensor
            def _(pe):
                pe.wait_ge(S["w_in"], 80)
                pe.wait_ge(S["small_in"], 96)
                pe.wait_ge(S["set_p"], 3)
                with pe.Fori(0, NTT) as t:
                    pe.wait_ge(S["mT_ready"], t + 1)
                    pe.wait_ge(S["x2_ready"], 1 + t)
                    for half in range(2):
                        for k in range(KD):
                            mm = pe.matmul(pX[:, half * 512:(half + 1) * 512], mT[:, k, :], w_out[:, k, half * 512:(half + 1) * 512], start=k == 0, stop=k == KD - 1)
                    mm.then_inc(S["x2_psum"], 1)
                    pe.wait_ge(S["h2_ready"], t + 1)
                    pe.wait_ge(S["shT_ready"], 1 + t)
                    for k in range(KD):
                        mm = pe.transpose(pT[:, k * P:(k + 1) * P], h2[:, k * P:(k + 1) * P], keep.ident[:, :])
                    mm.then_inc(S["hT_psum"], 1)
                    pe.wait_ge(S["hT_ready"], t + 1)
                    pe.wait_ge(S["count"], 1 + 3 * t)
                    for k in range(KD):
                        mm = pe.matmul(pR[:, 0:NE], hT[:, k, :], w_r[:, k, :], start=k == 0, stop=k == KD - 1)
                    mm.then_inc(S["route_psum"], 1)
                    pe.wait_ge(S["sh_ready"], 1 + 2 * t)
                    for k in range(KD):
                        mm = pe.matmul(pGU[:, :], hT[:, k, :], w_sgu[:, k, :], start=k == 0, stop=k == KD - 1)
                    mm.then_inc(S["route_psum"], 1)
                    pe.wait_ge(S["mask_ready"], t + 1)
                    pe.matmul(pR[:, 128:128 + NE], before[:, :], mask[:, :], start=True, stop=True)
                    pe.matmul(pR[:, 256:256 + NE], ones[:, :], mask[:, :], start=True, stop=True).then_inc(S["rank_psum"], 1)
                    pe.wait_ge(S["sh_ready"], 1 + 2 * t + 2)
                    for k in range(2):
                        mm = pe.transpose(pT[:, k * P:(k + 1) * P], sh[:, k * P:(k + 1) * P], keep.ident[:, :])
                    mm.then_inc(S["shT_psum"], 1)
                    pe.wait_ge(S["shT_ready"], 1 + t + 1)
                    pe.wait_ge(S["acc_ready"], 1 + t)
                    for half in range(2):
                        for k in range(2):
                            mm = pe.matmul(pD[:, half * 512:(half + 1) * 512], shT[:, k, :], w_sd[:, k, half * 512:(half + 1) * 512], start=k == 0, stop=k == 1)
                    mm.then_inc(S["down_psum"], 1)


def stage_experts(nc, a, o, keep):
    NTT = NT + 1
    CB = CAP - P
    W = 4
    Y0 = 8
    with Core(nc) as c:
        wgu = [c.sb(f"we_gu{p}", [P, KD, 2 * DE]) for p in range(2)]
        wd = [c.sb(f"we_d{p}", [P, 2, D]) for p in range(2)]
        xg = [c.sb(f"xg{p}", [P, 2, D]) for p in range(2)]
        xT = [c.sb(f"xT{p}", [P, KD, CAP]) for p in range(2)]
        yb = [c.sb(f"yb{p}", [P, 2, D]) for p in range(2)]
        slots = c.sb("slots", [P, CAP])
        trash = c.sb("trash", [P, 2])
        hot = c.sb("hot", [P, NTT, CAP], BF16)
        row = c.sb("row", [P, 2, 6])
        idxf = c.sb("idxf", [P, 2])
        idx = [c.sb(f"idx{i}", [P, 2], I32) for i in range(W)]
        wc = [c.sb(f"wc{i}", [P, 2]) for i in range(W)]
        sg = c.sb("sg", [P, 2, CAP])
        gs = c.sb("gs", [P, 2, CAP])
        h = c.sb("h_e", [P, 2, CAP])
        pT = [c.ps(f"pTe{i}") for i in range(2)]
        pY = [c.ps(f"pYe{i}") for i in range(2)]
        pG, pU, pI = c.ps("pGe"), c.ps("pUe"), c.ps("pIe")
        S = {n: c.sem("e_" + n) for n in """const_in cleared hot_ready tbl_psum steps idx_ready xT_psum xT_ready gu_psum
            sig_ready gate_ready h_ready y_psum y_vec y_act passed copied slots_moved rows_added""".split()}
        w_in = [c.sem(f"e_w_in{p}") for p in range(2)]
        x_in = [c.sem(f"e_x_in{p}") for p in range(2)]
        added = [c.sem(f"e_added{g}") for g in range(2)]

        def passes_of(eng):
            return eng.value_load(keep.passes[0:1, 0:1], min_val=1, max_val=-(-TOK // CAP))

        def over_experts(eng, start, body, end=None):
            n = passes_of(eng)
            with eng.Fori(0, n) as q:
                if start:
                    start(q)
                with eng.Fori(0, NE // W - 1) as j:
                    for r in range(W):
                        body(q, j, r, False)
                for r in range(W):
                    body(q, NE // W - 1, r, True)
                if end:
                    end(q)
            return n

        with c.block() as block:
            @block.sync
            def _(sp):
                sp.dma_start(slots[:, :], a["k_slots"]).then_inc(S["const_in"], 16)
                sp.dma_start(trash[:, :], a["k_trash"]).then_inc(S["const_in"], 16)

                def load(q, j, r, last):
                    e = W * j + r
                    p = r % 2
                    sp.wait_ge(S["y_psum"], 4 * (NE * q + e) + 4)
                    row_ = e if last else bass.ds(e, 1)
                    for dst, name in ((wgu[p][:, :, 0:DE], "w_e_gate"), (wgu[p][:, :, DE:2 * DE], "w_e_up"), (wd[p][:, :, :], "w_e_down")):
                        src = a[name][0][e:e + 1] if last else a[name][0][row_]
                        sp.dma_start(dst, src.rearrange("o (k p) n -> p (o k) n", p=P)).then_inc(w_in[p], 16)
                    if r == W - 1:
                        sp.sem_inc(S["passed"], 1)

                n = over_experts(sp, None, load)
                for g in range(2):
                    sp.wait_ge(added[g], n * (16 * NE))
                for i in range(4):
                    sp.dma_start(o["y_prompt"][i * 256:(i + 1) * 256, :], keep.acc_dram[i * 256:(i + 1) * 256, :]).then_inc(S["copied"], 16)
                sp.dma_start(o["y_sample"], keep.acc_dram[SEQ:TOK, :]).then_inc(S["copied"], 16)
                sp.wait_ge(S["copied"], 80)

            @block.gpsimd
            def _(pool):
                n_of = (P, CB)

                def gather(q, j, r):
                    u = NE * q + W * j + r
                    pool.wait_ge(S["idx_ready"], 1 + u + 1)
                    pool.wait_ge(S["xT_psum"], 1 + 4 * u)
                    pool.sem_inc(S["passed"], 1)
                    for g in range(2):
                        pool.indirect_dma_start(out=xg[r % 2][0:n_of[g], g, :], out_offset=None, in_=keep.h_dram[:, :],
                                                in_offset=bass.IndirectOffsetOnAxis(ap=idx[r % W][0:n_of[g], g:g + 1], axis=0)).then_inc(x_in[r % 2], 16)

                def start(q):
                    gather(q, 0, 0)
                    gather(q, 0, 1)

                def body(q, j, r, last):
                    u = NE * q + W * j + r
                    if not (last and r >= W - 2):
                        gather(q, j, r + 2)
                    for g in range(2):
                        pool.wait_ge(S["y_vec"], 1 + 2 * u + g + 1)
                        pool.wait_ge(S["y_act"], 1 + 2 * u + g + 1)
                        pool.sem_inc(S["passed"], 1)
                        pool.indirect_dma_start(out=keep.acc_dram[:, :], out_offset=bass.IndirectOffsetOnAxis(ap=idx[r][0:n_of[g], g:g + 1], axis=0),
                                                in_=yb[r % 2][0:n_of[g], g, :], in_offset=None, compute_op=ALU.add).then_inc(added[g], 16)
                    for g in range(2):
                        pool.wait_ge(added[g], 16 * u + 16)
                    pool.sem_inc(S["rows_added"], 1)

                over_experts(pool, start, body)

            @block.scalar
            def _(act):
                act.sem_inc(S["rows_added"], 1)
                act.sem_inc(S["xT_psum"], 4)
                c.start_at_one(act, S, "xT_psum rows_added tbl_psum idx_ready xT_ready h_ready y_vec y_act")
                def take(q, j, r):
                    u = NE * q + W * j + r
                    for s in range(4):
                        act.wait_ge(S["xT_psum"], 5 + 4 * u + s + 1)
                        act.activation(xT[r % 2][:, 2 * s:2 * s + 2, :], pT[s % 2][:, 0:2 * CAP].rearrange("p (k n) -> p k n", k=2), ACT.Copy).then_inc(S["xT_ready"], 1)

                def body(q, j, r, last):
                    u = NE * q + W * j + r
                    act.wait_ge(S["gu_psum"], u + 1)
                    act.activation(sg[:, :, :], pG[:, 0:2 * CAP].rearrange("p (f n) -> p f n", f=2), ACT.Sigmoid).then_inc(S["sig_ready"], 1)
                    if not (last and r == W - 1):
                        take(q, j, r + 1)
                    act.wait_ge(S["rows_added"], 1 + u)
                    for g in range(2):
                        n = (P, CB)[g]
                        act.wait_ge(S["y_psum"], Y0 + 4 * u + 2 * g + 2)
                        act.activation(yb[r % 2][0:n, g, 512:D], pY[1][0:n, :], ACT.Copy, scale=wc[r][0:n, g:g + 1]).then_inc(S["y_act"], 1)

                over_experts(act, lambda q: take(q, 0, 0), body)

            @block.vector
            def _(v):
                v.memset(pI[:, :], 0.0).then_inc(S["cleared"], 1)
                v.wait_ge(S["const_in"], 32)

                def table(q, j, r, last=False):
                    e = W * j + r
                    u = NE * q + e
                    v.wait_ge(S["tbl_psum"], 1 + u)
                    rank = keep.rank[:, :, e:e + 1] if isinstance(e, int) else keep.rank[:, :, bass.ds(e, 1)]
                    v.tensor_tensor(hot[:, :, :], spread(slots[:, :], NTT), rank.broadcast_to([P, NTT, CAP]), ALU.is_equal).then_inc(S["hot_ready"], 1)

                def rows(q, j, r):
                    u = NE * q + W * j + r
                    own = Steps(S["steps"], u, 4)
                    v.wait_ge(S["tbl_psum"], 1 + u + 1)
                    own.mark(v.tensor_copy(row[:, :, :], pI[:, 0:12].rearrange("p (g n) -> p g n", g=2)))
                    own.wait(v)
                    own.mark(v.scalar_tensor_tensor(row[:, :, 2], row[:, :, 2], -1.0, trash[:, :], ALU.add, ALU.mult))
                    own.wait(v)
                    v.tensor_reduce(wc[r % W][:, :], row[:, :, 3:6], AX.X, ALU.add)
                    own.mark(v.tensor_reduce(idxf[:, :], row[:, :, 0:3], AX.X, ALU.add))
                    own.wait(v)
                    own.mark(v.tensor_copy(idx[r % W][:, :], idxf[:, :]))
                    own.wait(v)
                    own.end()
                    v.sem_inc(S["idx_ready"], 1)

                def start(q):
                    table(q, 0, 0)
                    rows(q, 0, 0)
                    table(q, 0, 1)
                    rows(q, 0, 1)

                def body(q, j, r, last):
                    u = NE * q + W * j + r
                    ahead = not (last and r >= W - 2)
                    if ahead:
                        table(q, j, r + 2)
                    v.wait_ge(S["sig_ready"], u + 1)
                    v.tensor_tensor(gs[:, :, :], sg[:, :, :], pG[:, 0:2 * CAP].rearrange("p (f n) -> p f n", f=2), ALU.mult).then_inc(S["gate_ready"], 1)
                    v.wait_ge(S["gate_ready"], u + 1)
                    v.tensor_tensor(h[:, :, :], gs[:, :, :], pU[:, 0:2 * CAP].rearrange("p (f n) -> p f n", f=2), ALU.mult).then_inc(S["h_ready"], 1)
                    v.wait_ge(S["rows_added"], 1 + u)
                    if ahead:
                        rows(q, j, r + 2)
                    for g in range(2):
                        n = (P, CB)[g]
                        v.wait_ge(S["y_psum"], Y0 + 4 * u + 2 * g + 1)
                        v.tensor_scalar(yb[r % 2][0:n, g, 0:512], pY[0][0:n, :], wc[r][0:n, g:g + 1], None, ALU.mult).then_inc(S["y_vec"], 1)

                def end(q):
                    v.wait_ge(S["tbl_psum"], 1 + NE * q + NE)
                    v.tensor_scalar(slots[:, :], slots[:, :], float(CAP), None, ALU.add).then_inc(S["slots_moved"], 1)
                    v.wait_ge(S["slots_moved"], q + 1)

                over_experts(v, start, body, end)

            @block.tensor
            def _(pe):
                pe.sem_inc(S["y_psum"], Y0)
                pe.wait_ge(S["cleared"], 1)
                n_of = ((0, P), (P, CB))

                def table(q, j, r):
                    e = W * j + r
                    u = NE * q + e
                    pe.wait_ge(S["hot_ready"], u + 1)
                    pe.wait_ge(S["idx_ready"], 1 + u)
                    for g, (at, n) in enumerate(n_of):
                        for t in range(NTT):
                            col = keep.vals[:, t, :, e:e + 1] if isinstance(e, int) else keep.vals[:, t, :, bass.ds(e, 1)]
                            mm = pe.matmul(pI[0:n, 6 * g:6 * g + 6], hot[:, t, at:at + n], col.rearrange("p c o -> p (c o)"), start=t == 0, stop=t == NTT - 1)
                    mm.then_inc(S["tbl_psum"], 1)

                def turn(q, j, r, uses):
                    u = NE * q + W * j + r
                    pe.wait_ge(x_in[r % 2], 32 * uses + 32)
                    for s in range(4):
                        if s >= 2:
                            pe.wait_ge(S["xT_ready"], 1 + 4 * u + s - 1)
                        else:
                            pe.wait_ge(S["xT_ready"], 1 + 4 * u)
                        for k in range(2):
                            for g, (at, n) in enumerate(n_of):
                                kk = 2 * s + k
                                mm = pe.transpose(pT[s % 2][:, k * CAP + at:k * CAP + at + n], xg[r % 2][0:n, g, kk * P:(kk + 1) * P], keep.ident[0:n, 0:n])
                        mm.then_inc(S["xT_psum"], 1)

                def start(q):
                    table(q, 0, 0)
                    table(q, 0, 1)
                    turn(q, 0, 0, NE // 2 * q)

                def body(q, j, r, last):
                    u = NE * q + W * j + r
                    p = r % 2
                    uses = NE // 2 * q + W // 2 * j + r // 2
                    pe.wait_ge(w_in[p], 48 * uses + 48)
                    pe.wait_ge(S["xT_ready"], 1 + 4 * u + 4)
                    pe.wait_ge(S["h_ready"], 1 + u)
                    for dst, base in ((pG, 0), (pU, DE)):
                        for f in range(2):
                            for k in range(KD):
                                mm = pe.matmul(dst[:, f * CAP:(f + 1) * CAP], wgu[p][:, k, base + f * P:base + (f + 1) * P], xT[p][:, k, :], start=k == 0, stop=k == KD - 1)
                    mm.then_inc(S["gu_psum"], 1)
                    if not (last and r >= W - 2):
                        table(q, j, r + 2)
                    if not (last and r == W - 1):
                        turn(q, j, r + 1, NE // 2 * q + W // 2 * j + (r + 1) // 2)
                    pe.wait_ge(S["h_ready"], 1 + u + 1)
                    for g, (at, n) in enumerate(n_of):
                        for half in range(2):
                            pe.wait_ge(S["y_vec"] if half == 0 else S["y_act"], 1 + 2 * u + g)
                            for f in range(2):
                                mm = pe.matmul(pY[half][0:n, :], h[:, f, at:at + n], wd[p][:, f, half * 512:(half + 1) * 512], start=f == 0, stop=f == 1)
                            mm.then_inc(S["y_psum"], 1)

                over_experts(pe, start, body)


class Keep:
    pass


def program(nc, a, o):
    keep = Keep()
    keep.o_dram = nc.dram_tensor("attention_out", [NT, P, 2, 4 * P], F32, kind="Internal").ap()
    keep.h_dram = nc.dram_tensor("tokens_normed", [ROWS, D], F32, kind="Internal").ap()
    keep.acc_dram = nc.dram_tensor("sums", [ROWS, D], F32, kind="Internal").ap()
    with Core(nc) as top:
        keep.ident = top.sb("ident", [P, P])
        keep.mhalf = top.sb("minus_half", [P, 16])
        keep.mergedT = top.sb("mergedT", [P, KD, TOK])
        with Core(nc) as mid:
            keep.cos = mid.sb("cos", [P, NPAGE + 1, ROPE])
            keep.sin = mid.sb("sin", [P, NPAGE + 1, ROPE])
            keep.hT = mid.sb("hT", [P, KD, TOK])
            keep.mv = mid.sb("mv", [P, MT // P, MW])
            keep.mkT = mid.sb("mkT", [P, MH, MT])
            keep.qn = mid.sb("qn", [P, NHEAD * QH])
            keep.kn = mid.sb("kn", [P, NHEAD * QH])
            keep.ckv = mid.sb("ckv", [P, LORA])
            keep.kr = mid.sb("kr", [P, ROPE])
            keep.qmn = mid.sb("qmn", [P, MW])
            stage_constants(nc, a, keep)
            stage_memory(nc, a, o, keep)
            stage_tokens(nc, a, o, keep)
            keep.convT = mid.sb("convT", [P, KC, TOK])
            stage_conv(nc, a, o, keep)
            keep.oT_s = mid.sb("oT_s", [P, 4, DB])
            keep.moT_s = mid.sb("moT_s", [P, MH, DB])
            stage_sample(nc, a, o, keep)
            stage_merge(nc, a, keep)
        keep.rank = top.sb("rank", [P, NT + 1, NE])
        keep.vals = top.sb("vals", [P, NT + 1, 6, NE], BF16)
        keep.passes = top.sb("passes", [1, 1], I32)
        stage_mixer(nc, a, keep)
        stage_experts(nc, a, o, keep)


def constants():
    positions = np.arange((NPAGE + 1) * P)
    positions[PAST:] = PAST
    rates = (10000.0 ** (-np.arange(ROPE // 2, dtype=np.float32) / (ROPE // 2))).astype(np.float32)
    angles = positions.astype(np.float32)[:, None] * rates[None]
    cos, sin = np.cos(angles), np.sin(angles)
    row, column, tile = np.arange(P), np.arange(SEQ), np.arange(NT + 1)
    grid = np.zeros((P, NT + 1))
    made = dict(
        ident=np.eye(P),
        cos=np.concatenate([cos, cos], 1),
        sin=np.concatenate([sin, sin], 1),
        mask=np.where(column[None, :] <= column[:, None], 0.0, -1e30),
        before=np.triu(np.ones((P, P)), 1),
        valid=np.stack([np.ones(P), row < DB], 1),
        vals=np.stack([grid + P * tile[None], grid + row[:, None], grid + 1], 2),
        thresholds=(CAP * np.arange(-(-TOK // CAP)))[None],
        slots=np.broadcast_to(np.arange(CAP), (P, CAP)),
        trash=-np.stack([TOK + row, TOK + P + row], 1))
    return {"k_" + name: np.ascontiguousarray(table, dtype=np.float32) for name, table in made.items()}


_INS = ["x_prompt", "x_sample", "mem_prompt", "cache_latent", "cache_krope", "state_conv", "cache_mem_k", "cache_mem_v",
        "page_table", "g_attn_norm", "w_in", "g_q_lora", "w_uq", "g_q_mla", "g_kv_lora", "w_uk", "w_uv", "g_k_mla", "w_o_mla",
        "w_dw", "b_dw", "g_conv_ln", "b_conv_ln", "w_conv_out", "g_mem_norm", "w_mem_kv", "g_q_mem", "g_k_mem", "w_o_mem",
        "w_out", "g_ffn_norm", "w_router", "b_router", "w_e_gate", "w_e_up", "w_e_down", "w_s_gate", "w_s_up", "w_s_down"]
_OUTS = {
    "y_prompt": ((SEQ, D), (1, SEQ, D)), "y_sample": ((DB, D), (DB, 1, D)),
    "lat_p": ((SEQ, LORA), (1, 1, SEQ, LORA)), "kr_p": ((SEQ, ROPE), (1, 1, SEQ, ROPE)),
    "conv_p": ((HIST, CC), (1, 1, HIST, CC)),
    "mem_k": ((MT, MW), (1, 1, MT, MH, MHD)), "mem_v": ((MT, MW), (1, 1, MT, MH, MHD)),
    "lat_s": ((DB, LORA), (1, DB, 1, LORA)), "kr_s": ((DB, ROPE), (1, DB, 1, ROPE)),
    "conv_s": ((DB, HIST, CC), (1, DB, HIST, CC))}


def kernel(**inputs):
    import numpy as _np
    import concourse.bacc as _bacc
    from concourse import mybir as _mybir
    from concourse.bass_utils import run_bass_kernel_spmd as _run

    nc = _bacc.Bacc("TRN2", target_bir_lowering=False, num_devices=1)
    arrays, a, o = {}, {}, {}
    given = {name: _np.ascontiguousarray(inputs[name]) for name in _INS}
    given.update(constants())
    for name, x in given.items():
        arrays[f"in_{name}"] = x
        a[name] = nc.dram_tensor(f"in_{name}", x.shape, _mybir.dt.from_np(x.dtype), kind="ExternalInput").ap()
    for name, (shape, _) in _OUTS.items():
        o[name] = nc.dram_tensor(f"out_{name}", shape, F32, kind="ExternalOutput").ap()
    program(nc, a, o)
    r = _run(nc, [arrays], core_ids=[0])
    return tuple(r.results[0][f"out_{name}"].reshape(shape) for name, (_, shape) in _OUTS.items())
```
